# Optimizing a Trainium2 kernel written in Bass

```python
import jax, jax.numpy as jnp
from jax import lax
import numpy as np

D_MODEL = 2048
BATCH = 1
SEQ = 256
DEPTH = 1

MLA_HEADS = 8
MLA_Q_RANK = 512
MLA_KV_RANK = 256
MLA_NOPE_DIM = 128
MLA_ROPE_DIM = 64
MLA_V_DIM = 128
MLA_QK_DIM = MLA_NOPE_DIM + MLA_ROPE_DIM
MLA_Q_BLOCK = 128
MOBA_HEADS = 8
MOBA_HEAD_DIM = 128
MOBA_BLOCK = 256
MOBA_TOPK = 3
MOBA_Q_CHUNK = 32
MLA_WIDTH = MLA_HEADS * MLA_V_DIM
MOBA_WIDTH = MOBA_HEADS * MOBA_HEAD_DIM
MIX_WIDTH = MLA_WIDTH + MOBA_WIDTH
IN_SPLITS = (MLA_Q_RANK, MLA_KV_RANK, MLA_ROPE_DIM, MOBA_WIDTH, MOBA_WIDTH, MOBA_WIDTH)
IN_PROJ_DIM = sum(IN_SPLITS)
FFN_DIM = 5632
ROPE_THETA = 10000.0
NORM_EPS = 1e-6
NEG_INF = -1e30

kernel_name = "hymba_mla_moba_macaron_block"

def rms_norm(x, g):
    xf = x.astype(jnp.float32)
    y = xf * lax.rsqrt(jnp.mean(xf * xf, axis=-1, keepdims=True) + NORM_EPS)
    return (y * g.astype(jnp.float32)).astype(x.dtype)

def rope_tables(seq, dim):
    inv = 1.0 / (ROPE_THETA ** (jnp.arange(0, dim, 2, dtype=jnp.float32) / dim))
    ang = jnp.arange(seq, dtype=jnp.float32)[:, None] * inv[None, :]
    return jnp.cos(ang), jnp.sin(ang)

def apply_rope(x, cos, sin):
    half = x.shape[-1] // 2
    x1, x2 = x[..., :half], x[..., half:]
    c = cos.astype(x.dtype)
    s = sin.astype(x.dtype)
    return jnp.concatenate([x1 * c - x2 * s, x2 * c + x1 * s], axis=-1)

def swiglu(x, w_gate, w_up, w_down):
    return (jax.nn.silu(x @ w_gate) * (x @ w_up)) @ w_down

def mla_attention(c_q, c_kv, k_rope_raw, g_q, g_kv, w_uq, w_ukv):
    B, S, _ = c_q.shape
    H = MLA_HEADS
    q = (rms_norm(c_q, g_q) @ w_uq).reshape(B, S, H, MLA_QK_DIM).transpose(0, 2, 1, 3)
    kv = (rms_norm(c_kv, g_kv) @ w_ukv).reshape(B, S, H, MLA_NOPE_DIM + MLA_V_DIM).transpose(0, 2, 1, 3)
    q_nope, q_pe = q[..., :MLA_NOPE_DIM], q[..., MLA_NOPE_DIM:]
    k_nope, v = kv[..., :MLA_NOPE_DIM], kv[..., MLA_NOPE_DIM:]
    cos, sin = rope_tables(S, MLA_ROPE_DIM)
    q_pe = apply_rope(q_pe, cos, sin)
    k_pe = apply_rope(k_rope_raw[:, None], cos, sin)
    q = jnp.concatenate([q_nope, q_pe], axis=-1)
    k = jnp.concatenate([k_nope, jnp.broadcast_to(k_pe, (B, H, S, MLA_ROPE_DIM))], axis=-1)
    scale = MLA_QK_DIM ** -0.5
    nq = S // MLA_Q_BLOCK
    qb = q.reshape(B, H, nq, MLA_Q_BLOCK, MLA_QK_DIM).transpose(2, 0, 1, 3, 4)
    key_pos = jnp.arange(S)

    def block(args):
        qi, i = args
        s = jnp.einsum('bhqd,bhkd->bhqk', qi, k).astype(jnp.float32) * scale
        qpos = i * MLA_Q_BLOCK + jnp.arange(MLA_Q_BLOCK)
        s = jnp.where(key_pos[None, :] <= qpos[:, None], s, NEG_INF)
        p = jax.nn.softmax(s, axis=-1).astype(v.dtype)
        return jnp.einsum('bhqk,bhkd->bhqd', p, v)

    out = lax.map(block, (qb, jnp.arange(nq)))
    return out.transpose(1, 0, 3, 2, 4).reshape(B, S, H * MLA_V_DIM)

def moba_attention(q, k, v):
    B, S, _ = q.shape
    H, D, L = MOBA_HEADS, MOBA_HEAD_DIM, MOBA_BLOCK
    q = q.reshape(B, S, H, D).transpose(0, 2, 1, 3)
    k = k.reshape(B, S, H, D).transpose(0, 2, 1, 3)
    v = v.reshape(B, S, H, D).transpose(0, 2, 1, 3)
    cos, sin = rope_tables(S, D)
    q = apply_rope(q, cos, sin)
    k = apply_rope(k, cos, sin)
    nb = -(-S // L)
    pad = nb * L - S
    kp = jnp.pad(k, ((0, 0), (0, 0), (0, pad), (0, 0)))
    vp = jnp.pad(v, ((0, 0), (0, 0), (0, pad), (0, 0)))
    kb = kp.reshape(B, H, nb, L, D)
    vb = vp.reshape(B, H, nb, L, D)
    k_mean = jnp.mean(kb.astype(jnp.float32), axis=3)
    gate = jnp.einsum('bhsd,bhnd->bhsn', q.astype(jnp.float32), k_mean)
    q_blk = jnp.arange(S) // L
    past = jnp.arange(nb)[None, :] < q_blk[:, None]
    gate = jnp.where(past, gate, NEG_INF)
    n_sel = max(1, min(MOBA_TOPK, nb - 1))
    _, sel = lax.top_k(gate, n_sel)
    sel_valid = jnp.arange(n_sel)[None, :] < q_blk[:, None]
    gather = jax.vmap(jax.vmap(lambda blocks, idx: blocks[idx]))
    scale = D ** -0.5
    nc = S // MOBA_Q_CHUNK

    def chunk(c):
        t0 = c * MOBA_Q_CHUNK
        qc = lax.dynamic_slice_in_dim(q, t0, MOBA_Q_CHUNK, axis=2)
        idx = lax.dynamic_slice_in_dim(sel, t0, MOBA_Q_CHUNK, axis=2)
        valid = lax.dynamic_slice_in_dim(sel_valid, t0, MOBA_Q_CHUNK, axis=0)
        kg = gather(kb, idx)
        vg = gather(vb, idx)
        own0 = (t0 // L) * L
        k_own = lax.dynamic_slice_in_dim(kp, own0, L, axis=2)
        v_own = lax.dynamic_slice_in_dim(vp, own0, L, axis=2)
        s_sel = jnp.einsum('bhqd,bhqkld->bhqkl', qc, kg).astype(jnp.float32) * scale
        s_sel = jnp.where(valid[None, None, :, :, None], s_sel, NEG_INF)
        s_sel = s_sel.reshape(B, H, MOBA_Q_CHUNK, n_sel * L)
        s_own = jnp.einsum('bhqd,bhld->bhql', qc, k_own).astype(jnp.float32) * scale
        qpos = t0 + jnp.arange(MOBA_Q_CHUNK)
        kpos = own0 + jnp.arange(L)
        s_own = jnp.where(kpos[None, :] <= qpos[:, None], s_own, NEG_INF)
        p = jax.nn.softmax(jnp.concatenate([s_sel, s_own], axis=-1), axis=-1).astype(v.dtype)
        p_sel = p[..., :n_sel * L].reshape(B, H, MOBA_Q_CHUNK, n_sel, L)
        p_own = p[..., n_sel * L:]
        return (jnp.einsum('bhqkl,bhqkld->bhqd', p_sel, vg)
                + jnp.einsum('bhql,bhld->bhqd', p_own, v_own))

    out = lax.map(chunk, jnp.arange(nc))
    return out.transpose(1, 0, 3, 2, 4).reshape(B, S, H * D)

def setup_inputs(seed: int = 0) -> dict:
    key = jax.random.key(seed)
    ks = jax.random.split(key, 24)

    def w(k, fan_in, fan_out):
        return jax.random.normal(k, (DEPTH, fan_in, fan_out), jnp.float32) * fan_in ** -0.5

    def g(k, n):
        return 1.0 + 0.02 * jax.random.normal(k, (DEPTH, n), jnp.float32)

    return {
        "x": jax.random.normal(ks[0], (BATCH, SEQ, D_MODEL), jnp.float32),
        "ffn1_pre_g": g(ks[1], D_MODEL),
        "ffn1_w_gate": w(ks[2], D_MODEL, FFN_DIM),
        "ffn1_w_up": w(ks[3], D_MODEL, FFN_DIM),
        "ffn1_w_down": w(ks[4], FFN_DIM, D_MODEL),
        "ffn1_post_g": g(ks[5], D_MODEL),
        "mix_pre_g": g(ks[6], D_MODEL),
        "w_in": w(ks[7], D_MODEL, IN_PROJ_DIM),
        "mla_q_norm_g": g(ks[8], MLA_Q_RANK),
        "mla_kv_norm_g": g(ks[9], MLA_KV_RANK),
        "mla_w_uq": w(ks[10], MLA_Q_RANK, MLA_HEADS * MLA_QK_DIM),
        "mla_w_ukv": w(ks[11], MLA_KV_RANK, MLA_HEADS * (MLA_NOPE_DIM + MLA_V_DIM)),
        "mla_out_g": g(ks[12], MLA_WIDTH),
        "moba_out_g": g(ks[13], MOBA_WIDTH),
        "w_out": w(ks[14], MIX_WIDTH, D_MODEL),
        "mix_post_g": g(ks[15], D_MODEL),
        "ffn2_pre_g": g(ks[16], D_MODEL),
        "ffn2_w_gate": w(ks[17], D_MODEL, FFN_DIM),
        "ffn2_w_up": w(ks[18], D_MODEL, FFN_DIM),
        "ffn2_w_down": w(ks[19], FFN_DIM, D_MODEL),
        "ffn2_post_g": g(ks[20], D_MODEL),
    }

def reference(x, ffn1_pre_g, ffn1_w_gate, ffn1_w_up, ffn1_w_down, ffn1_post_g,
              mix_pre_g, w_in, mla_q_norm_g, mla_kv_norm_g, mla_w_uq, mla_w_ukv,
              mla_out_g, moba_out_g, w_out, mix_post_g,
              ffn2_pre_g, ffn2_w_gate, ffn2_w_up, ffn2_w_down, ffn2_post_g):
    cuts = list(np.cumsum(IN_SPLITS)[:-1])
    for l in range(DEPTH):
        h = swiglu(rms_norm(x, ffn1_pre_g[l]), ffn1_w_gate[l], ffn1_w_up[l], ffn1_w_down[l])
        x = x + 0.5 * rms_norm(h, ffn1_post_g[l])
        u = rms_norm(x, mix_pre_g[l])
        c_q, c_kv, k_rope, q_m, k_m, v_m = jnp.split(u @ w_in[l], cuts, axis=-1)
        a = mla_attention(c_q, c_kv, k_rope, mla_q_norm_g[l], mla_kv_norm_g[l],
                          mla_w_uq[l], mla_w_ukv[l])
        m = moba_attention(q_m, k_m, v_m)
        y = jnp.concatenate([rms_norm(a, mla_out_g[l]), rms_norm(m, moba_out_g[l])], axis=-1) @ w_out[l]
        x = x + rms_norm(y, mix_post_g[l])
        h = swiglu(rms_norm(x, ffn2_pre_g[l]), ffn2_w_gate[l], ffn2_w_up[l], ffn2_w_down[l])
        x = x + 0.5 * rms_norm(h, ffn2_post_g[l])
    return x


_drawn_inputs = setup_inputs


def setup_inputs(seed=0):
    import zlib

    import numpy as np

    out = dict(_drawn_inputs(seed))
    spreads = {}
    factors = {'ffn1_pre_g': 3.056,
     'ffn1_post_g': 4.423,
     'mla_q_norm_g': 6.387,
     'mla_kv_norm_g': 4.056,
     'mla_out_g': 22.667,
     'moba_out_g': 21.73,
     'mix_post_g': 10.629,
     'ffn2_pre_g': 19.875,
     'ffn2_post_g': 35.069}
    for name, (base, spread) in spreads.items():
        noise = np.random.default_rng([zlib.crc32(name.encode()), seed]).standard_normal(out[name].shape)
        drawn = base * np.exp(spread * noise) if base else spread * noise
        out[name] = __import__('jax').numpy.asarray(drawn.astype(out[name].dtype))
    for name, factor in factors.items():
        out[name] = (out[name] * factor).astype(out[name].dtype)
    return out
```

```python
from collections import namedtuple
from contextlib import ExitStack

import numpy as np

import concourse.bass as bass
from concourse import mybir

P = 128
TILES = 2
TOKENS = P * TILES
D = 2048
DC = D // P
FFN = 5632
FB = 256
N_FB = FFN // FB
FC = FFN // P
HEADS = 8
HD = 128
ROPE = 64
Q_RANK, KV_RANK = 512, 256
QC, KVC = Q_RANK // P, KV_RANK // P
BANK = 512
RAW = 4
PIECE = 2048
EPS = 1e-6
MASKED = -1e30
MOBA_SCALE = float(HD) ** -0.5
MLA_SCALE = float(HD + ROPE) ** -0.5

IN_BLOCKS, UQ_BLOCKS, UKV_BLOCKS, OUT_BLOCKS = 8, 4, 4, 4
GU1 = 0
DOWN1 = GU1 + 4 * N_FB
IN = DOWN1 + FC
UQ = IN + 4 * IN_BLOCKS
UKV = UQ + UQ_BLOCKS
OUT = UKV + UKV_BLOCKS // 2
GU2 = OUT + 4 * OUT_BLOCKS
DOWN2 = GU2 + 4 * N_FB
HALF = FC // 2

B_GU1 = 0
B_IN = B_GU1 + N_FB
B_UQ = B_IN + IN_BLOCKS
B_UKV = B_UQ + UQ_BLOCKS
B_OUT = B_UKV + UKV_BLOCKS
B_GU2 = B_OUT

T_GU1 = 0
T_CKV = T_GU1 + N_FB
T_CQ = T_CKV + 1
T_QK = T_CQ + 1
T_UQ = T_QK + 4
T_UKV = T_UQ + UQ_BLOCKS
T_GU2 = T_UKV + UKV_BLOCKS

K_GU1 = T_GU1
K_QK, K_UQ, K_UKV, K_GU2 = T_QK - 1, T_UQ - 1, T_UKV - 1, T_GU2 - 1

G_Q, G_KV = 4 * DC, 4 * DC + QC
G_ROWS = 4 * DC + QC + KVC

MOBA_TAB, MLA_TAB = 3 * HD // 2, 3 * ROPE // 2

(R_PRE1, R_POST1, R_PRE_MIX, R_KV, R_Q, R_MOBA, R_MLA, R_POST_MIX, R_PRE2, R_POST2) = range(10)

ALU = mybir.AluOpType
ACT = mybir.ActivationFunctionType
F32 = mybir.dt.float32
F32R = mybir.dt.float32r
BF16 = mybir.dt.bfloat16

Piece = namedtuple("Piece", "index slot fills split")


def piece(first, i=0, step=0):
    return Piece(first + step * i, first % RAW, first // RAW + (step // RAW) * i, first % 2)


def build_layer(nc, x, ffn1_pre_g, ffn1_w_gate, ffn1_w_up, ffn1_w_down, ffn1_post_g,
                mix_pre_g, w_in, mla_q_norm_g, mla_kv_norm_g, mla_w_uq, mla_w_ukv,
                mla_out_g, moba_out_g, w_out, mix_post_g,
                ffn2_pre_g, ffn2_w_gate, ffn2_w_up, ffn2_w_down, ffn2_post_g, rope, out):
    ctx = ExitStack()
    with ctx:
        def sb(name, shape, dt=F32, stack=ctx):
            return stack.enter_context(nc.sbuf_tensor(name, shape, dt))

        def sem(name):
            return ctx.enter_context(nc.semaphore(name))

        rows = sb("rows", [P, TILES, D])
        raw = sb("raw", [P, RAW, PIECE])
        w_hi = sb("w_hi", [P, 2, PIECE], F32R)
        w_lo = sb("w_lo", [P, 2, PIECE], F32R)
        gain_row = sb("gain_row", [P, D])
        ident = sb("ident", [P, P])
        mask = sb("mask", [P, 2 * P])
        gain_in = sb("gain_in", [G_ROWS, P])
        gain = sb("gain", [P, G_ROWS])
        tab = sb("tab", [P, TILES, MOBA_TAB + MLA_TAB])
        probs = sb("probs", [P, 2, 3 * P])
        sumsq = sb("sumsq", [P, TILES, 4])
        var = sb("var", [P, 10, TILES])
        rs = sb("rs", [P, 10, TILES])
        minus_half = sb("minus_half", [P, TILES])
        peak = sb("peak", [P, 2, TILES])
        shift = sb("shift", [P, 2, TILES])
        total = sb("total", [P, 2, TILES])
        rtotal = sb("rtotal", [P, 2, TILES])

        with ExitStack() as s:
            act_hi = sb("act_hi", [P, DC, TOKENS], F32R, s)
            act_lo = sb("act_lo", [P, DC, TOKENS], F32R, s)
        q2T = sb("q2T", [P, HEADS, TOKENS])
        k2T = sb("k2T", [P, HEADS, TOKENS])
        q2pT = sb("q2pT", [ROPE, HEADS, TOKENS])
        v2 = sb("v2", [P, TILES, HEADS * HD])

        with ExitStack() as s:
            hidT = sb("hidT", [P, FC, TOKENS], F32, s)
        qkT = sb("qkT", [P, 2 * HEADS, TOKENS])
        v1 = sb("v1", [P, TILES, HEADS * HD])
        heads = sb("heads", [P, TILES, D])
        k2pT = sb("k2pT", [ROPE, TOKENS])
        tab_r = sb("tab_r", [P, TILES, MOBA_TAB])
        tab_q = sb("tab_q", [P, TILES, MLA_TAB])
        sb("hid_pad", [P, 192])

        with ExitStack() as s:
            hid_split = sb("hid_split", [P, 2, 2, 2, TOKENS], F32R, s)
            silu = sb("silu", [P, TILES, FB], F32, s)
            hid = sb("hid", [P, TILES, FB], F32, s)
        with ExitStack() as s:
            sb("junk_at", [P, 2, 2, 2, TOKENS], F32, s)
            junk = sb("junk", [P, D], BF16, s)
        lat_hi = sb("lat_hi", [P, QC + KVC, TOKENS], F32R)
        lat_lo = sb("lat_lo", [P, QC + KVC, TOKENS], F32R)

        with ExitStack() as s:
            scaled = sb("scaled", [P, TILES, D], F32, s)
        with ExitStack() as s:
            lat = sb("lat", [P, TILES, Q_RANK + KV_RANK + ROPE], F32, s)
        masked = sb("masked", [P, 2, 3 * P])
        probsT = sb("probsT", [P, 2, 3 * P])
        sb("lat_pad", [P, 128])
        turn_in = sb("turn_in", [P, TILES, BANK])
        rot_a = sb("rot_a", [P, BANK])
        rot_b = sb("rot_b", [P, BANK])
        sb("scaled_pad", [P, 384])
        junk_mix = probs[:, 0, 0:256].bitcast(BF16)

        banks = ctx.enter_context(nc.psum_tensor("banks", [P, 8, BANK], F32))

        rows_landed = [sem(f"rows_landed{k}") for k in range(4)]
        gains_landed = sem("gains_landed")
        tab_landed = sem("tab_landed")
        gain_row_landed = sem("gain_row_landed")
        raw_landed = [sem(f"raw_landed{s}") for s in range(RAW)]
        stored = sem("stored")
        zeroed = sem("zeroed")
        consts_made = sem("consts_made")
        gains_turned = sem("gains_turned")
        gains_kept = sem("gains_kept")
        hi_ready = sem("hi_ready")
        lo_ready = sem("lo_ready")
        piece_used = sem("piece_used")
        rows_ready = sem("rows_ready")
        quad_turned = sem("quad_turned")
        act_hi_ready = sem("act_hi_ready")
        act_ready = sem("act_ready")
        squared = sem("squared")
        var_ready = sem("var_ready")
        rs_ready = sem("rs_ready")
        silu_ready = sem("silu_ready")
        taken = sem("taken")
        turned = sem("turned")
        kept = sem("kept")
        tab_scaled = sem("tab_scaled")
        rot_step = sem("rot_step")
        pe_rows = sem("pe_rows")
        lat_hi_ready = sem("lat_hi_ready")
        lat_ready = sem("lat_ready")
        kv_half = sem("kv_half")
        y_scaled = sem("y_scaled")
        scores_ready = sem("scores_ready")
        peaked = sem("peaked")
        shifted = sem("shifted")
        probs_ready = sem("probs_ready")
        probs_turned = sem("probs_turned")
        probs_kept = sem("probs_kept")
        head_ready = sem("head_ready")
        totalled = sem("totalled")
        head_out = sem("head_out")

        x_dram = x.rearrange("b (t p) d -> p (b t) d", p=P)
        out_dram = out.rearrange("b (t p) d -> p (b t) d", p=P)

        def by_chunk(w):
            return w.rearrange("l (c p) n -> p (l c) n", p=P)

        w_gate = {GU1: by_chunk(ffn1_w_gate), GU2: by_chunk(ffn2_w_gate)}
        w_up = {GU1: by_chunk(ffn1_w_up), GU2: by_chunk(ffn2_w_up)}
        w_down = {DOWN1: by_chunk(ffn1_w_down), DOWN2: by_chunk(ffn2_w_down)}
        in_w, uq_w, ukv_w, out_w = by_chunk(w_in), by_chunk(mla_w_uq), by_chunk(mla_w_ukv), by_chunk(w_out)

        def cut(t, slot, chunks, width):
            return t[:, slot, 0:chunks * width].rearrange("p (c n) -> p c n", c=chunks)

        def result(block, t):
            return banks[:, 2 * (block % 2) + t, :]

        def tile_of(t):
            return slice(t * P, (t + 1) * P)

        def quarter(k):
            return slice(k * BANK, (k + 1) * BANK)

        def down_banks(half, t):
            return ((6, 0), (2, 4))[half][t]

        def turn_bank(k, j):
            return (6, 4)[k % 2] + j // 2

        def turn_at(k, j):
            return banks[:, turn_bank(k, j), (j % 2) * TOKENS:(j % 2 + 1) * TOKENS]

        in_width = [KV_RANK + ROPE] + [BANK] * 7
        in_col = [Q_RANK, 0] + [Q_RANK + KV_RANK + ROPE + BANK * n for n in range(6)]

        block = ctx.enter_context(nc.Block())

        @block.sync
        def _(sp):
            def raw_free(pc):
                if not (isinstance(pc.index, int) and pc.index < RAW):
                    sp.wait_ge(lo_ready, pc.index - RAW + 1)

            def load_gate_up(stage, b, pc, i):
                raw_free(pc)
                to = cut(raw, pc.slot, 4, 2 * FB)
                cols = bass.ds(b * FB, FB)
                sp.dma_start(to[:, :, 0:FB], w_gate[stage][:, 4 * i:4 * i + 4, cols]).then_inc(raw_landed[pc.slot], 16)
                sp.dma_start(to[:, :, FB:], w_up[stage][:, 4 * i:4 * i + 4, cols]).then_inc(raw_landed[pc.slot], 16)

            def load_gate_up_all(stage):
                with sp.Fori(1, N_FB) as b:
                    for i in range(4):
                        load_gate_up(stage, b, piece(stage + i, b, 4), i)

            def load_down(stage, half, n, pc):
                raw_free(pc)
                to = cut(raw, pc.slot, 2, D // 2)
                for j in range(2):
                    sp.dma_start(to[:, j:j + 1, :], w_down[stage][:, bass.ds(2 * n + j, 1),
                                 half * D // 2:(half + 1) * D // 2]).then_inc(raw_landed[pc.slot], 16)

            def load_down_all(stage):
                for half in range(2):
                    at = stage + half * HALF
                    for n in range(2):
                        load_down(stage, half, n, piece(at + n))
                    with sp.Fori(0, (HALF - 2) // 4) as i:
                        for n in range(2, 6):
                            load_down(stage, half, 4 * i + n, piece(at + n, i, 4))

            def load_block(w, pc, chunk, chunks, col, width):
                raw_free(pc)
                to = cut(raw, pc.slot, chunks, width)
                for a in range(0, chunks, chunks // 2):
                    sp.dma_start(to[:, a:a + chunks // 2, :],
                                 w[:, chunk + a:chunk + a + chunks // 2, bass.ds(col, width)])\
                      .then_inc(raw_landed[pc.slot], 16)

            for i in range(4):
                load_gate_up(GU1, 0, piece(GU1 + i), i)
            load_gate_up_all(GU1)
            load_down_all(DOWN1)
            for b in range(3):
                for i in range(4):
                    load_block(in_w, piece(IN + 4 * b + i), 4 * i, 4, in_col[b], in_width[b])
            sp.wait_ge(y_scaled, 4)
            sp.dma_start(gain_row[:, :], mix_post_g.rearrange("l d -> (l d)").partition_broadcast(P))\
              .then_inc(gain_row_landed, 16)
            with sp.Fori(3, IN_BLOCKS) as b:
                for i in range(4):
                    load_block(in_w, piece(IN + i, b, 4), 4 * i, 4, b * BANK + (in_col[2] - 2 * BANK), BANK)
            for b in range(UQ_BLOCKS):
                load_block(uq_w, piece(UQ + b), 0, QC, 2 * b * (HD + ROPE), 2 * (HD + ROPE))
            for b in range(2):
                load_block(ukv_w, piece(UKV + b), 0, KVC, b * 2 * BANK, 2 * BANK)
            with sp.Fori(0, OUT_BLOCKS) as b:
                for i in range(4):
                    load_block(out_w, piece(OUT + i, b, 4), 4 * i, 4, b * BANK, BANK)
            for i in range(4):
                load_gate_up(GU2, 0, piece(GU2 + i), i)
            sp.wait_ge(y_scaled, 4 + 2 * OUT_BLOCKS)
            sp.dma_start(gain_row[:, :], ffn2_post_g.rearrange("l d -> (l d)").partition_broadcast(P))\
              .then_inc(gain_row_landed, 16)
            load_gate_up_all(GU2)
            load_down_all(DOWN2)
            for k in range(4):
                for t in range(TILES):
                    sp.wait_ge(rows_ready, 24 + 2 * k + t + 1)
                    sp.dma_start(out_dram[:, t, quarter(k)], rows[:, t, quarter(k)]).then_inc(stored, 16)
            sp.wait_ge(stored, 16 * 4 * TILES)

        @block.gpsimd
        def _(pool):
            nc.gpsimd.memset(ident[:, :], 0.0)
            nc.gpsimd.memset(mask[:, :], 0.0)
            nc.gpsimd.memset(minus_half[:, :], -0.5).then_inc(zeroed, 1)
            pool.wait_ge(zeroed, 1)
            nc.gpsimd.affine_select(out=ident[:, :], in_=ident[:, :], compare_op=ALU.not_equal, fill=1.0,
                                    base=0, pattern=[[-1, P]], channel_multiplier=1)
            nc.gpsimd.affine_select(out=mask[:, P:2 * P], in_=mask[:, P:2 * P], compare_op=ALU.is_ge,
                                    fill=MASKED, base=0, pattern=[[-1, P]], channel_multiplier=1)\
              .then_inc(consts_made, 1)

            steps = [0]

            def inverse_rms(job, sums, parts, width, factor, col=0):
                pool.wait_ge(squared, sums)
                for n in range(1, parts):
                    nc.gpsimd.tensor_tensor(sumsq[:, :, 0], sumsq[:, :, 0], sumsq[:, :, n], ALU.add)\
                      .then_inc(var_ready, 1)
                    steps[0] += 1
                    pool.wait_ge(var_ready, steps[0])
                c = factor ** -2
                nc.gpsimd.tensor_scalar(var[:, job, :], sumsq[:, :, col], c / width, c * EPS, ALU.mult, ALU.add)\
                  .then_inc(var_ready, 1)
                steps[0] += 1
                pool.wait_ge(var_ready, steps[0])
                nc.gpsimd.tensor_tensor(rs[:, job, :], var[:, job, :], minus_half[:, :], ALU.pow)\
                  .then_inc(rs_ready, 1)

            inverse_rms(R_PRE1, 2, 1, D, 1.0)
            inverse_rms(R_POST1, 6, 2, D, 0.5)
            inverse_rms(R_PRE_MIX, 8, 1, D, 1.0)
            inverse_rms(R_KV, 10, 1, KV_RANK, 1.0, col=2)
            inverse_rms(R_Q, 12, 1, Q_RANK, 1.0, col=3)
            inverse_rms(R_MOBA, 14, 1, HEADS * HD, 1.0, col=0)
            inverse_rms(R_MLA, 16, 1, HEADS * HD, 1.0, col=1)
            inverse_rms(R_POST_MIX, 24, 4, D, 1.0)
            inverse_rms(R_PRE2, 26, 1, D, 1.0)
            inverse_rms(R_POST2, 30, 2, D, 0.5)

        @block.scalar
        def _(act):
            def take_high(pc, width=PIECE):
                act.wait_ge(raw_landed[pc.slot], 32 * (pc.fills + 1))
                if not (isinstance(pc.index, int) and pc.index < 2):
                    act.wait_ge(piece_used, pc.index - 1)
                nc.scalar.activation(w_hi[:, pc.split, 0:width], raw[:, pc.slot, 0:width], ACT.Copy)\
                  .then_inc(hi_ready, 1)

            def turn_high(turn, k):
                act.wait_ge(quad_turned, 4 * turn + k + 1)
                for j in range(4):
                    c = 4 * k + j
                    nc.scalar.activation(act_hi[:, c, :], turn_at(k, j), ACT.Copy,
                                         scale=gain[:, DC * turn + c:DC * turn + c + 1]).then_inc(act_hi_ready, 1)

            squares = [0]

            def square(of, scratch, tile, col):
                if squares[0]:
                    act.wait_ge(squared, squares[0])
                nc.scalar.activation(scratch, of, ACT.Square, accum_out=sumsq[:, tile, col:col + 1])\
                  .then_inc(squared, 1)
                squares[0] += 1

            def square_rows():
                for t in range(TILES):
                    square(rows[:, t, :], junk[:, :], t, 0)

            def silu_block(stage, b):
                first = B_GU1 if stage == GU1 else B_GU2
                if not (isinstance(b, int) and b == 0):
                    act.wait_ge(taken, 2 * first + 2 * b)
                job = R_PRE1 if stage == GU1 else R_PRE2
                return first, job

            def gate(stage, b, parity):
                first, job = silu_block(stage, b)
                for t in range(TILES):
                    nc.scalar.activation(silu[:, t, :], result(parity, t)[:, 0:FB], ACT.Silu,
                                         scale=rs[:, job, t:t + 1]).then_inc(silu_ready, 1)

            def keep_hidden(stage, b):
                first = T_GU1 if stage == GU1 else T_GU2
                act.wait_ge(turned, first + b + 1)
                nc.scalar.copy(hidT[:, bass.ds(2 * b, 2), :],
                               banks[:, 4, :].rearrange("p (c n) -> p c n", c=2)).then_inc(kept, 1)

            def gate_up(stage, turn):
                for i in range(4):
                    if not (turn and i < 2):
                        take_high(piece(stage + i))
                    if i < 2:
                        turn_high(turn, i)
                    elif i == 2:
                        turn_high(turn, 2)
                        turn_high(turn, 3)
                        square_rows()
                act.wait_ge(rs_ready, (R_PRE1 if stage == GU1 else R_PRE2) + 1)
                take_high(piece(stage + 4))
                take_high(piece(stage + 5))
                gate(stage, 0, 0)
                take_high(piece(stage + 6))
                take_high(piece(stage + 7))
                keep_hidden(stage, 0)
                with act.Fori(0, (N_FB - 2) // 2) as n:
                    for e in range(2):
                        for i in range(4):
                            take_high(piece(stage + 8 + 4 * e + i, n, 8))
                            if i == 1:
                                gate(stage, 2 * n + (e + 1), (e + 1) % 2)
                        keep_hidden(stage, 2 * n + (e + 1))

            def take_high_down(pc, n):
                act.wait_ge(raw_landed[pc.slot], 32 * (pc.fills + 1))
                act.wait_ge(piece_used, pc.index - 1)
                nc.scalar.copy(hid_split[:, pc.split, 0], hidT[:, bass.ds(2 * n, 2), :])
                nc.scalar.activation(w_hi[:, pc.split, :], raw[:, pc.slot, :], ACT.Copy).then_inc(hi_ready, 1)

            def square_down(half, scaled_before):
                for t in range(TILES):
                    if t == 1:
                        act.wait_ge(y_scaled, scaled_before + 1)
                    b = down_banks(half, t)
                    square(banks[:, b:b + 2, :].rearrange("p b n -> p (b n)"), junk[:, 0:D // 2], t, half)

            def down(gu_stage, stage, scaled_before):
                take_high_down(piece(stage), 0)
                take_high_down(piece(stage + 1), 1)
                gate(gu_stage, N_FB - 1, 1)
                keep_hidden(gu_stage, N_FB - 1)
                with act.Fori(0, (HALF - 2) // 4) as i:
                    for n in range(2, 6):
                        take_high_down(piece(stage + n, i, 4), 4 * i + n)
                take_high_down(piece(stage + HALF), 0)
                take_high_down(piece(stage + HALF + 1), 1)
                square_down(0, scaled_before)
                with act.Fori(0, (HALF - 2) // 4) as i:
                    for n in range(2, 6):
                        take_high_down(piece(stage + HALF + n, i, 4), 4 * i + n)

            def keep_qk(j):
                act.wait_ge(turned, T_QK + 1 + j)
                for t in range(TILES):
                    ins = nc.scalar.copy(qkT[:, bass.ds(4 * j, 4), tile_of(t)],
                                         banks[:, 4 + t, :].rearrange("p (h n) -> p h n", h=4))
                ins.then_inc(kept, 1)

            def latent_high(first, chunks, bank, g):
                for c in range(chunks):
                    nc.scalar.activation(lat_hi[:, first + c, :],
                                         banks[:, bank + c // 2, (c % 2) * TOKENS:(c % 2 + 1) * TOKENS],
                                         ACT.Copy, scale=gain[:, g + c:g + c + 1]).then_inc(lat_hi_ready, 1)

            def square_latent(tiles_taken, cols, col):
                act.wait_ge(taken, tiles_taken)
                for t in range(TILES):
                    square(lat[:, t, cols], junk_mix[:, 0:cols.stop - cols.start], t, col)

            def keep_q2(j):
                act.wait_ge(turned, T_UQ + j + 1)
                for t in range(TILES):
                    b = banks[:, 4 + t, :].rearrange("p (h n) -> p h n", h=4)
                    nc.scalar.copy(q2T[:, 2 * j:2 * j + 2, tile_of(t)], b[:, 0:2, :])
                    ins = nc.scalar.copy(q2pT[:, 2 * j:2 * j + 2, tile_of(t)], b[0:ROPE, 2:4, :])
                ins.then_inc(kept, 1)

            def keep_k2(j):
                act.wait_ge(turned, T_UKV + j + 1)
                for t in range(TILES):
                    b = banks[:, 4 + t, :].rearrange("p (h n) -> p h n", h=4)
                    ins = nc.scalar.copy(k2T[:, 2 * j:2 * j + 2, tile_of(t)], b[:, 0:2, :])
                ins.then_inc(kept, 1)

            def mix_in():
                turn_high(1, 0)
                turn_high(1, 1)
                take_high(piece(IN + 2), 4 * in_width[0])
                turn_high(1, 2)
                turn_high(1, 3)
                square_rows()
                take_high(piece(IN + 3), 4 * in_width[0])
                take_high(piece(IN + 4))
                take_high(piece(IN + 5))
                square_latent(2 * B_IN + 2, slice(Q_RANK, Q_RANK + KV_RANK), 2)
                take_high(piece(IN + 6))
                take_high(piece(IN + 7))
                act.wait_ge(turned, T_CKV + 1)
                latent_high(QC, KVC, 6, G_KV)
                nc.scalar.copy(k2pT[:, :], banks[0:ROPE, 7, 0:TOKENS]).then_inc(kept, 1)
                take_high(piece(IN + 8))
                take_high(piece(IN + 9))
                square_latent(2 * B_IN + 4, slice(0, Q_RANK), 3)
                take_high(piece(IN + 10))
                take_high(piece(IN + 11))
                act.wait_ge(turned, T_CQ + 1)
                latent_high(0, QC, 4, G_Q)
                with act.Fori(0, 2) as n:
                    for e in range(2):
                        for i in range(4):
                            take_high(piece(IN + 12 + 4 * e + i, n, 8))
                        keep_qk(2 * n + e)
                for i in range(4):
                    take_high(piece(IN + 28 + i))

            def latent_up():
                uq_width = QC * 2 * (HD + ROPE)
                take_high(piece(UQ), uq_width)
                take_high(piece(UQ + 1), uq_width)
                take_high(piece(UQ + 2), uq_width)
                keep_q2(0)
                take_high(piece(UQ + 3), uq_width)
                keep_q2(1)
                take_high(piece(UKV))
                keep_q2(2)
                take_high(piece(UKV + 1))
                keep_q2(3)
                keep_k2(0)
                take_high(piece(OUT))
                keep_k2(1)
                keep_k2(2)
                take_high(piece(OUT + 1))
                keep_k2(3)

            def attention():
                for u in range(2 * HEADS + 1):
                    if u < 2 * HEADS:
                        a = u % 2
                        scale = MOBA_SCALE if u < HEADS else MLA_SCALE
                        act.wait_ge(shifted, u + 1)
                        if u >= 2:
                            act.wait_ge(probs_turned, u - 1)
                            act.wait_ge(totalled, u - 1)
                        nc.scalar.activation(probs[:, a, 0:P], masked[:, a, 0:P], ACT.Exp, bias=shift[:, a, 0:1],
                                             scale=scale, accum_out=total[:, a, 0:1])
                        nc.scalar.activation(probs[:, a, P:], masked[:, a, P:], ACT.Exp, bias=shift[:, a, 1:2],
                                             scale=scale, accum_out=total[:, a, 1:2]).then_inc(probs_ready, 1)
                    if u >= 1:
                        a = (u - 1) % 2
                        act.wait_ge(probs_turned, u)
                        if u >= 3:
                            act.wait_ge(head_ready, u - 2)
                        nc.scalar.copy(probsT[:, a, :], banks[:, 2 + a, 0:3 * P]).then_inc(probs_kept, 1)
                    if u == HEADS + 3:
                        square_heads(1, HEADS)
                square_heads(0, 2 * HEADS)

            def square_heads(half, done):
                act.wait_ge(head_out, done)
                for t in range(TILES):
                    square(heads[:, t, half * D // 2:(half + 1) * D // 2], rot_a[:, :].bitcast(BF16), t, 1 - half)

            def square_out(n):
                act.wait_ge(piece_used, OUT + 4 * n + 4)
                for t in range(TILES):
                    if t == 1:
                        act.wait_ge(y_scaled, 4 + 2 * n + 1)
                    square(result(n, t), junk[:, 0:BANK], t, n)

            def mix_out():
                turn_high(2, 0)
                turn_high(2, 1)
                take_high(piece(OUT + 2))
                turn_high(2, 2)
                turn_high(2, 3)
                take_high(piece(OUT + 3))
                for n in range(1, OUT_BLOCKS):
                    take_high(piece(OUT + 4 * n))
                    take_high(piece(OUT + 4 * n + 1))
                    square_out(n - 1)
                    take_high(piece(OUT + 4 * n + 2))
                    take_high(piece(OUT + 4 * n + 3))
                take_high(piece(GU2))
                square_out(OUT_BLOCKS - 1)
                take_high(piece(GU2 + 1))

            act.dma_start(rows[:, :, quarter(0)], x_dram[:, :, quarter(0)]).then_inc(rows_landed[0], 16)
            at = 0
            for g in (ffn1_pre_g, mix_pre_g, mla_out_g, moba_out_g, ffn2_pre_g, mla_q_norm_g, mla_kv_norm_g):
                n = g.shape[1] // P
                act.dma_start(gain_in[at:at + n, :], g.rearrange("l (r p) -> (l r) p", p=P)).then_inc(gains_landed, 16)
                at += n
            for k in range(1, 4):
                act.dma_start(rows[:, :, quarter(k)], x_dram[:, :, quarter(k)]).then_inc(rows_landed[k], 16)
            act.dma_start(tab[:, :, :], rope.rearrange("(t p) n -> p t n", p=P)).then_inc(tab_landed, 16)
            act.dma_start(gain_row[:, :], ffn1_post_g.rearrange("l d -> (l d)").partition_broadcast(P))\
               .then_inc(gain_row_landed, 16)
            act.wait_ge(gains_turned, 1)
            nc.scalar.copy(gain[:, :], banks[:, 7, 256:256 + G_ROWS]).then_inc(gains_kept, 1)
            act.wait_ge(gains_kept, 1)

            gate_up(GU1, 0)
            down(GU1, DOWN1, 0)
            take_high(piece(IN), 4 * in_width[0])
            act.wait_ge(piece_used, IN)
            square_down(1, 2)
            take_high(piece(IN + 1), 4 * in_width[0])
            mix_in()
            latent_up()
            attention()
            mix_out()
            gate_up(GU2, 3)
            down(GU2, DOWN2, 4 + 2 * OUT_BLOCKS)
            act.wait_ge(piece_used, DOWN2 + FC)
            square_down(1, 4 + 2 * OUT_BLOCKS + 2)

        @block.vector
        def _(dve):
            def take_low(pc, width=PIECE):
                dve.wait_ge(hi_ready, pc.index + 1)
                nc.vector.tensor_tensor(w_lo[:, pc.split, 0:width], raw[:, pc.slot, 0:width],
                                        w_hi[:, pc.split, 0:width], ALU.subtract).then_inc(lo_ready, 1)

            def turn_low(turn, k):
                for j in range(4):
                    c = 4 * k + j
                    if j % 2 == 0:
                        dve.wait_ge(act_hi_ready, DC * turn + c + 2)
                    nc.vector.scalar_tensor_tensor(
                        out=act_lo[:, c, :], in0=turn_at(k, j), scalar=gain[:, DC * turn + c:DC * turn + c + 1],
                        in1=act_hi[:, c, :], op0=ALU.mult, op1=ALU.subtract).then_inc(act_ready, 1)

            def multiply_hidden(stage, b, parity):
                blocks, turns, job = ((B_GU1, T_GU1, R_PRE1) if stage == GU1 else (B_GU2, T_GU2, R_PRE2))
                if not (isinstance(b, int) and b == 0):
                    dve.wait_ge(turned, turns + b)
                for t in range(TILES):
                    dve.wait_ge(silu_ready, b * 2 + (2 * turns_before(stage) + t + 1))
                    nc.vector.scalar_tensor_tensor(
                        out=hid[:, t, :], in0=result(parity, t)[:, FB:], scalar=rs[:, job, t:t + 1],
                        in1=silu[:, t, :], op0=ALU.mult, op1=ALU.mult).then_inc(taken, 1)

            def turns_before(stage):
                return 0 if stage == GU1 else N_FB

            def add_residual(job, turn):
                for k in range(4):
                    for t in range(TILES):
                        if k == 0 and t == 0:
                            dve.wait_ge(rs_ready, job + 1)
                            dve.wait_ge(y_scaled, scaled_parts[job])
                        nc.vector.scalar_tensor_tensor(
                            out=rows[:, t, quarter(k)], in0=scaled[:, t, quarter(k)], scalar=rs[:, job, t:t + 1],
                            in1=rows[:, t, quarter(k)], op0=ALU.mult, op1=ALU.add).then_inc(rows_ready, 1)
                    if turn is not None and k >= 1:
                        turn_low(turn, k - 1)
                if turn is not None:
                    turn_low(turn, 3)

            scaled_parts = {R_POST1: 4, R_POST_MIX: 4 + 2 * OUT_BLOCKS, R_POST2: 8 + 2 * OUT_BLOCKS}

            def gate_up(stage):
                for i in range(2, 4):
                    take_low(piece(stage + i))
                dve.wait_ge(rs_ready, (R_PRE1 if stage == GU1 else R_PRE2) + 1)
                take_low(piece(stage + 4))
                take_low(piece(stage + 5))
                multiply_hidden(stage, 0, 0)
                take_low(piece(stage + 6))
                take_low(piece(stage + 7))
                with dve.Fori(0, (N_FB - 2) // 2) as n:
                    for e in range(2):
                        for i in range(4):
                            take_low(piece(stage + 8 + 4 * e + i, n, 8))
                            if i == 1:
                                multiply_hidden(stage, 2 * n + (e + 1), (e + 1) % 2)

            def take_low_down(pc, n, kept_all=None):
                dve.wait_ge(hi_ready, pc.index + 1)
                nc.vector.tensor_tensor(hid_split[:, pc.split, 1], hidT[:, bass.ds(2 * n, 2), :],
                                        hid_split[:, pc.split, 0], ALU.subtract)
                nc.vector.tensor_tensor(w_lo[:, pc.split, :], raw[:, pc.slot, :], w_hi[:, pc.split, :],
                                        ALU.subtract).then_inc(lo_ready, 1)

            def scale_down(half, sums_before):
                for t in (1, 0):
                    if t == 0:
                        dve.wait_ge(squared, sums_before + 1)
                    b = down_banks(half, t)
                    cols = slice(half * D // 2, (half + 1) * D // 2)
                    nc.vector.tensor_tensor(scaled[:, t, cols], banks[:, b:b + 2, :].rearrange("p b n -> p (b n)"),
                                            gain_row[:, cols], ALU.mult).then_inc(y_scaled, 1)

            def down(gu_stage, stage, sums_before, gain_loads):
                take_low_down(piece(stage), 0)
                take_low_down(piece(stage + 1), 1)
                multiply_hidden(gu_stage, N_FB - 1, 1)
                with dve.Fori(0, (HALF - 2) // 4) as i:
                    for n in range(2, 6):
                        take_low_down(piece(stage + n, i, 4), 4 * i + n)
                take_low_down(piece(stage + HALF), 0)
                take_low_down(piece(stage + HALF + 1), 1)
                dve.wait_ge(piece_used, stage + HALF)
                dve.wait_ge(gain_row_landed, 16 * gain_loads)
                scale_down(0, sums_before)
                with dve.Fori(0, (HALF - 2) // 4) as i:
                    for n in range(2, 6):
                        take_low_down(piece(stage + HALF + n, i, 4), 4 * i + n)

            rotations = [0]

            def rotate(to, of, table, n_heads, half, wait_first=True):
                def by_head(ap):
                    return ap.rearrange("p (h a d) -> p h a d", h=n_heads, a=2)
                n = n_heads * 2 * half
                a, b = by_head(rot_a[:, 0:n]), by_head(rot_b[:, 0:n])

                def bc(lo, reps):
                    shape = [P, n_heads] + reps + [half]
                    t = table[:, lo:lo + half].unsqueeze(1)
                    if reps:
                        t = t.unsqueeze(1)
                    return t.to_broadcast(shape)
                nc.vector.tensor_tensor(a, of, bc(0, [2]), ALU.mult)
                nc.vector.tensor_tensor(b[:, :, 0, :], of[:, :, 1, :], bc(half, []), ALU.mult)
                nc.vector.tensor_tensor(b[:, :, 1, :], of[:, :, 0, :], bc(2 * half, []), ALU.mult)\
                  .then_inc(rot_step, 1)
                return a, b, to

            def rotate_done(a, b, to, count):
                dve.wait_ge(rot_step, count)
                return nc.vector.tensor_tensor(to, a, b, ALU.add)

            def rotate_qk(j, parity):
                dve.wait_ge(piece_used, j * 4 + (IN + 4 * 3))
                dve.wait_ge(turned, T_QK + j)
                for t in range(TILES):
                    if t == 1:
                        dve.wait_ge(taken, j * 2 + (2 * (B_IN + 2) + 1))
                    of = result(parity, t).rearrange("p (h a d) -> p h a d", h=4, a=2)
                    to = turn_in[:, t, :].rearrange("p (h a d) -> p h a d", h=4, a=2)
                    a, b, to = rotate(to, of, tab_r[:, t, :], 4, HD // 2)
                    rotate_done(a, b, to, j * 2 + (2 + t + 1)).then_inc(taken, 1)

            def scale_latent(b, width, at):
                dve.wait_ge(piece_used, IN + 4 * (b + 1))
                for t in range(TILES):
                    nc.vector.tensor_scalar(lat[:, t, at:at + width], result(b, t)[:, 0:width],
                                            rs[:, R_PRE_MIX, t:t + 1], None, ALU.mult).then_inc(taken, 1)

            def latent_low(first, chunks, bank, g):
                for c in range(chunks):
                    if c % 2 == 0:
                        dve.wait_ge(lat_hi_ready, lat_order(first) + c + 2)
                    nc.vector.scalar_tensor_tensor(
                        out=lat_lo[:, first + c, :],
                        in0=banks[:, bank + c // 2, (c % 2) * TOKENS:(c % 2 + 1) * TOKENS],
                        scalar=gain[:, g + c:g + c + 1], in1=lat_hi[:, first + c, :],
                        op0=ALU.mult, op1=ALU.subtract).then_inc(lat_ready, 1)

            def lat_order(first):
                return 0 if first == QC else KVC

            def scale_v1(n, parity):
                dve.wait_ge(piece_used, IN + 4 * (7 + n))
                for t in range(TILES):
                    nc.vector.tensor_scalar(v1[:, t, quarter(n)], result(parity, t),
                                            rs[:, R_PRE_MIX, t:t + 1], None, ALU.mult).then_inc(taken, 1)

            def mix_in():
                for i in range(2, 4):
                    take_low(piece(IN + i), 4 * in_width[0])
                take_low(piece(IN + 4))
                take_low(piece(IN + 5))
                dve.wait_ge(rs_ready, R_PRE_MIX + 1)
                dve.wait_ge(tab_landed, 16)
                for t in range(TILES):
                    nc.vector.tensor_scalar(tab_r[:, t, :], tab[:, t, 0:MOBA_TAB], rs[:, R_PRE_MIX, t:t + 1],
                                            None, ALU.mult).then_inc(tab_scaled, 1)
                scale_latent(0, in_width[0], Q_RANK)
                dve.wait_ge(taken, 2 * B_IN + 2)
                for t in range(TILES):
                    at = Q_RANK + KV_RANK
                    if t == 1:
                        dve.wait_ge(pe_rows, 1)
                    of = lat[:, t, at:at + ROPE].rearrange("p (h a d) -> p h a d", h=1, a=2)
                    to = turn_in[:, t, 0:ROPE].rearrange("p (h a d) -> p h a d", h=1, a=2)
                    a, b, to = rotate(to, of, tab[:, t, MOBA_TAB:], 1, ROPE // 2)
                    rotate_done(a, b, to, t + 1).then_inc(pe_rows, 1)
                take_low(piece(IN + 6))
                take_low(piece(IN + 7))
                latent_low(QC, KVC, 6, G_KV)
                take_low(piece(IN + 8))
                take_low(piece(IN + 9))
                scale_latent(1, Q_RANK, 0)
                take_low(piece(IN + 10))
                take_low(piece(IN + 11))
                latent_low(0, QC, 4, G_Q)
                dve.wait_ge(tab_scaled, 2)
                with dve.Fori(0, 2) as n:
                    for e in range(2):
                        for i in range(4):
                            take_low(piece(IN + 12 + 4 * e + i, n, 8))
                            if i == 1:
                                rotate_qk(2 * n + e, e)
                take_low(piece(IN + 28))
                take_low(piece(IN + 29))
                scale_v1(0, 0)
                take_low(piece(IN + 30))
                take_low(piece(IN + 31))

            def split_q2(j):
                dve.wait_ge(piece_used, UQ + j + 1)
                dve.wait_ge(turned, T_UQ + j)
                for t in range(TILES):
                    if t == 1:
                        dve.wait_ge(taken, 2 * (B_UQ + j) + 1)
                    of = result(j, t)[:, 0:2 * (HD + ROPE)].rearrange("p (h n) -> p h n", h=2)
                    nc.vector.tensor_scalar(turn_in[:, t, 0:2 * HD].rearrange("p (h n) -> p h n", h=2),
                                            of[:, :, 0:HD], rs[:, R_Q, t:t + 1], None, ALU.mult)
                    to = turn_in[:, t, 2 * HD:2 * HD + 2 * ROPE].rearrange("p (h a d) -> p h a d", h=2, a=2)
                    a, b, to = rotate(to, of[:, :, HD:].rearrange("p h (a d) -> p h a d", a=2),
                                      tab_q[:, t, :], 2, ROPE // 2)
                    rotate_done(a, b, to, 10 + 2 * j + t + 1).then_inc(taken, 1)

            def split_kv2(j):
                dve.wait_ge(turned, T_UKV + j)
                if j % 2 == 0:
                    dve.wait_ge(kv_half, j // 2 + 1)
                else:
                    dve.wait_ge(piece_used, UKV + j // 2 + 1)
                for t in range(TILES):
                    of = result(j, t).rearrange("p (h n) -> p h n", h=2)
                    nc.vector.tensor_scalar(turn_in[:, t, 0:2 * HD].rearrange("p (h n) -> p h n", h=2),
                                            of[:, :, 0:HD], rs[:, R_KV, t:t + 1], None, ALU.mult)
                    nc.vector.tensor_scalar(v2[:, t, 2 * j * HD:(2 * j + 2) * HD].rearrange("p (h n) -> p h n", h=2),
                                            of[:, :, HD:], rs[:, R_KV, t:t + 1], None, ALU.mult).then_inc(taken, 1)

            def latent_up():
                uq_width = QC * 2 * (HD + ROPE)
                dve.wait_ge(rs_ready, R_Q + 1)
                for t in range(TILES):
                    nc.vector.tensor_scalar(tab_q[:, t, :], tab[:, t, MOBA_TAB:], rs[:, R_Q, t:t + 1],
                                            None, ALU.mult).then_inc(tab_scaled, 1)
                take_low(piece(UQ), uq_width)
                take_low(piece(UQ + 1), uq_width)
                scale_v1(1, 1)
                dve.wait_ge(tab_scaled, 4)
                split_q2(0)
                take_low(piece(UQ + 2), uq_width)
                split_q2(1)
                take_low(piece(UQ + 3), uq_width)
                split_q2(2)
                take_low(piece(UKV))
                split_q2(3)
                take_low(piece(UKV + 1))
                split_kv2(0)
                split_kv2(1)
                take_low(piece(OUT))
                split_kv2(2)
                split_kv2(3)
                take_low(piece(OUT + 1))

            def attention():
                for u in range(2 * HEADS + 2):
                    if u < 2 * HEADS:
                        a = u % 2
                        scale = MOBA_SCALE if u < HEADS else MLA_SCALE
                        s = banks[:, a, :]
                        dve.wait_ge(scores_ready, u + 1)
                        if u >= 2:
                            dve.wait_ge(probs_ready, u - 1)
                        nc.vector.tensor_tensor_reduce(
                            out=masked[:, a, 0:P], in0=s[:, 0:P], in1=mask[:, P:], scale=1.0, scalar=3 * MASKED,
                            op0=ALU.add, op1=ALU.max, accum_out=peak[:, a, 0:1])
                        nc.vector.tensor_tensor_reduce(
                            out=masked[:, a, P:], in0=s[:, P:3 * P], in1=mask[:, :], scale=1.0, scalar=3 * MASKED,
                            op0=ALU.add, op1=ALU.max, accum_out=peak[:, a, 1:2]).then_inc(peaked, 1)
                        dve.wait_ge(peaked, u + 1)
                        nc.vector.tensor_scalar(shift[:, a, :], peak[:, a, :], -scale, None, ALU.mult)\
                          .then_inc(shifted, 1)
                    if u >= 2:
                        v = u - 2
                        a = v % 2
                        at = (D // 2 if v < HEADS else 0) + (v % HEADS) * HD
                        dve.wait_ge(probs_ready, v + 1)
                        nc.vector.reciprocal(rtotal[:, a, :], total[:, a, :]).then_inc(totalled, 1)
                        dve.wait_ge(totalled, v + 1)
                        dve.wait_ge(head_ready, v + 1)
                        for t in range(TILES):
                            ins = nc.vector.tensor_scalar(heads[:, t, at:at + HD], banks[:, 4 + a, tile_of(t)],
                                                          rtotal[:, a, t:t + 1], None, ALU.mult)
                        ins.then_inc(head_out, 1)

            def mix_out():
                dve.wait_ge(rs_ready, R_MLA + 1)
                dve.wait_ge(head_out, 2 * HEADS)
                for k in range(4):
                    for t in range(TILES):
                        job = R_MLA if k < 2 else R_MOBA
                        nc.vector.tensor_scalar(heads[:, t, quarter(k)], heads[:, t, quarter(k)],
                                                rs[:, job, t:t + 1], None, ALU.mult).then_inc(rows_ready, 1)
                    if k >= 1:
                        turn_low(2, k - 1)
                turn_low(2, 3)
                take_low(piece(OUT + 2))
                take_low(piece(OUT + 3))
                dve.wait_ge(gain_row_landed, 32)
                for n in range(1, OUT_BLOCKS):
                    take_low(piece(OUT + 4 * n))
                    take_low(piece(OUT + 4 * n + 1))
                    scale_out(n - 1)
                    take_low(piece(OUT + 4 * n + 2))
                    take_low(piece(OUT + 4 * n + 3))
                take_low(piece(GU2))
                scale_out(OUT_BLOCKS - 1)
                take_low(piece(GU2 + 1))

            def scale_out(n):
                dve.wait_ge(piece_used, OUT + 4 * n + 4)
                for t in (1, 0):
                    if t == 0:
                        dve.wait_ge(squared, 16 + 2 * n + 1)
                    nc.vector.tensor_tensor(scaled[:, t, quarter(n)], result(n, t), gain_row[:, quarter(n)],
                                            ALU.mult).then_inc(y_scaled, 1)

            dve.wait_ge(gains_kept, 1)
            take_low(piece(GU1))
            turn_low(0, 0)
            take_low(piece(GU1 + 1))
            turn_low(0, 1)
            turn_low(0, 2)
            turn_low(0, 3)
            gate_up(GU1)
            down(GU1, DOWN1, 2, 1)
            take_low(piece(IN), 4 * in_width[0])
            dve.wait_ge(piece_used, IN)
            scale_down(1, 4)
            take_low(piece(IN + 1), 4 * in_width[0])
            add_residual(R_POST1, 1)
            mix_in()
            latent_up()
            attention()
            mix_out()
            add_residual(R_POST_MIX, 3)
            gate_up(GU2)
            down(GU2, DOWN2, 26, 3)
            dve.wait_ge(piece_used, DOWN2 + FC)
            scale_down(1, 28)
            add_residual(R_POST2, None)

        @block.tensor
        def _(pe):
            def three_passes(out_ap, hi, lo, rhs_hi, rhs_lo, start, stop, chain=False):
                nc.tensor.matmul(out_ap, hi, rhs_hi, start=start, stop=False, skip_group_check=chain)
                nc.tensor.matmul(out_ap, hi, rhs_lo, start=False, stop=False, skip_group_check=chain)
                return nc.tensor.matmul(out_ap, lo, rhs_hi, start=False, stop=stop, skip_group_check=chain)

            def turn(n_turn, k):
                source = heads if n_turn == 2 else rows
                if k >= 2:
                    pe.wait_ge(act_ready, DC * n_turn + 4 * (k - 1))
                for t in range(TILES):
                    if n_turn == 0:
                        pe.wait_ge(rows_landed[k], 16)
                    else:
                        pe.wait_ge(rows_ready, 8 * (n_turn - 1) + 2 * k + t + 1)
                    for j in range(4):
                        c = 4 * k + j
                        mm = nc.tensor.transpose(turn_at(k, j)[:, tile_of(t)],
                                                 source[:, t, c * P:(c + 1) * P], ident[:, :])
                mm.then_inc(quad_turned, 1)

            def dense_piece(pc, i, blk, parity, width=BANK, n_turn=None):
                pe.wait_ge(lo_ready, pc.index + 1)
                if i == 0 and not (isinstance(blk, int) and blk in (B_GU1, B_GU1 + 1)):
                    pe.wait_ge(taken, blk * 2 - 2)
                rhs_hi, rhs_lo = cut(w_hi, pc.split, 4, width), cut(w_lo, pc.split, 4, width)
                for j in range(4):
                    c = 4 * i + j
                    if n_turn is not None:
                        pe.wait_ge(act_ready, DC * n_turn + c + 1)
                    for t in range(TILES):
                        mm = three_passes(result(parity, t)[:, 0:width], act_hi[:, c, tile_of(t)],
                                          act_lo[:, c, tile_of(t)], rhs_hi[:, j, :], rhs_lo[:, j, :],
                                          start=(c == 0), stop=(c == DC - 1))
                mm.then_inc(piece_used, 1)

            def first_block(at, blk, n_turn, width=BANK):
                turn(n_turn, 0)
                turn(n_turn, 1)
                dense_piece(piece(at), 0, blk, 0, width, n_turn)
                turn(n_turn, 2)
                dense_piece(piece(at + 1), 1, blk, 0, width, n_turn)
                turn(n_turn, 3)
                dense_piece(piece(at + 2), 2, blk, 0, width, n_turn)
                dense_piece(piece(at + 3), 3, blk, 0, width, n_turn)

            def turn_hidden(stage, b):
                blocks, keeps = ((B_GU1, K_GU1) if stage == GU1 else (B_GU2, K_GU2))
                if not (isinstance(b, int) and b == 0):
                    pe.wait_ge(kept, keeps + b)
                pe.wait_ge(taken, b * 2 + (2 * blocks + 2))
                for c in range(2):
                    for t in range(TILES):
                        mm = nc.tensor.transpose(banks[:, 4, c * TOKENS + t * P:c * TOKENS + (t + 1) * P],
                                                 hid[:, t, tile_of(c)], ident[:, :])
                mm.then_inc(turned, 1)

            def gate_up(stage, n_turn):
                blocks = B_GU1 if stage == GU1 else B_GU2
                first_block(stage, blocks, n_turn)
                for i in range(4):
                    dense_piece(piece(stage + 4 + i), i, blocks + 1, 1)
                    if i == 1:
                        turn_hidden(stage, 0)
                with pe.Fori(0, (N_FB - 2) // 2) as n:
                    for e in range(2):
                        for i in range(4):
                            dense_piece(piece(stage + 8 + 4 * e + i, n, 8), i, n * 2 + (blocks + 2 + e), e)
                            if i == 1:
                                turn_hidden(stage, n * 2 + (1 + e))

            def down_piece(pc, half):
                pe.wait_ge(lo_ready, pc.index + 1)
                rhs_hi, rhs_lo = cut(w_hi, pc.split, 2, D // 2), cut(w_lo, pc.split, 2, D // 2)
                for j in range(2):
                    for t in range(TILES):
                        b = down_banks(half, t)
                        hi = hid_split[:, pc.split, 0, j, tile_of(t)]
                        lo = hid_split[:, pc.split, 1, j, tile_of(t)]
                        for lhs, rhs in ((hi, rhs_hi), (hi, rhs_lo), (lo, rhs_hi)):
                            for n in range(2):
                                mm = nc.tensor.matmul(banks[:, b + n, :], lhs, rhs[:, j, quarter(n)],
                                                      start=False, stop=True, skip_group_check=True)
                mm.then_inc(piece_used, 1)

            def open_banks(half):
                for t in range(TILES):
                    for n in range(2):
                        nc.tensor.matmul(banks[:, down_banks(half, t) + n, 0:2], mask[:, 0:P], mask[:, 0:2],
                                         start=True, stop=True, skip_group_check=True)

            def down(gu_stage, stage):
                blocks, keeps = ((B_GU1, K_GU1) if gu_stage == GU1 else (B_GU2, K_GU2))
                pe.wait_ge(taken, 2 * blocks + 2 * (N_FB - 1))
                open_banks(0)
                down_piece(piece(stage), 0)
                turn_hidden(gu_stage, N_FB - 1)
                down_piece(piece(stage + 1), 0)
                with pe.Fori(0, (HALF - 2) // 4) as i:
                    for n in range(2, 6):
                        down_piece(piece(stage + n, i, 4), 0)
                pe.wait_ge(kept, keeps + N_FB)
                open_banks(1)
                for n in range(2):
                    down_piece(piece(stage + HALF + n), 1)
                with pe.Fori(0, (HALF - 2) // 4) as i:
                    for n in range(2, 6):
                        down_piece(piece(stage + HALF + n, i, 4), 1)

            def turn_latent(first, chunks, bank, col, count):
                pe.wait_ge(taken, count)
                for c in range(chunks):
                    for t in range(TILES):
                        mm = nc.tensor.transpose(banks[:, bank + c // 2, (c % 2) * TOKENS + t * P:
                                                       (c % 2) * TOKENS + (t + 1) * P],
                                                 lat[:, t, col + c * P:col + (c + 1) * P], ident[:, :])
                return mm

            def turn_qk(j):
                pe.wait_ge(taken, j * 2 + (2 * (B_IN + 2) + 2))
                pe.wait_ge(kept, K_QK + j)
                for t in range(TILES):
                    for h in range(4):
                        mm = nc.tensor.transpose(banks[:, 4 + t, tile_of(h)], turn_in[:, t, tile_of(h)], ident[:, :])
                mm.then_inc(turned, 1)

            def mix_in():
                first_block(IN, B_IN, 1, in_width[0])
                for i in range(4):
                    dense_piece(piece(IN + 4 + i), i, B_IN + 1, 1)
                    if i == 1:
                        pe.wait_ge(act_ready, 2 * DC)
                        turn_latent(QC, KVC, 6, Q_RANK, 2 * B_IN + 2)
                        pe.wait_ge(pe_rows, 2)
                        for t in range(TILES):
                            mm = nc.tensor.transpose(banks[0:ROPE, 7, tile_of(t)], turn_in[:, t, 0:ROPE], ident[:, :])
                        mm.then_inc(turned, 1)
                for i in range(4):
                    dense_piece(piece(IN + 8 + i), i, B_IN + 2, 0)
                    if i == 1:
                        turn_latent(0, QC, 4, 0, 2 * B_IN + 4).then_inc(turned, 1)
                pe.wait_ge(lat_ready, QC + KVC)
                with pe.Fori(0, 2) as n:
                    for e in range(2):
                        for i in range(4):
                            dense_piece(piece(IN + 12 + 4 * e + i, n, 8), i, n * 2 + (B_IN + 3 + e), 1 - e)
                            if i == 1:
                                turn_qk(2 * n + e)
                for i in range(4):
                    dense_piece(piece(IN + 28 + i), i, B_IN + 7, 1)

            def latent_block(pc, blk, first, chunks, rhs, width):
                pe.wait_ge(lo_ready, pc.index + 1)
                pe.wait_ge(taken, 2 * blk - 2)
                rhs_hi, rhs_lo = rhs
                for c in range(chunks):
                    for t in range(TILES):
                        mm = three_passes(result(blk, t)[:, 0:width], lat_hi[:, first + c, tile_of(t)],
                                          lat_lo[:, first + c, tile_of(t)], rhs_hi[:, c, :], rhs_lo[:, c, :],
                                          start=(c == 0), stop=(c == chunks - 1))
                return mm

            def turn_q2(j):
                pe.wait_ge(taken, 2 * (B_UQ + j) + 2)
                pe.wait_ge(kept, K_UQ + j)
                for t in range(TILES):
                    for h in range(2):
                        nc.tensor.transpose(banks[:, 4 + t, tile_of(h)], turn_in[:, t, tile_of(h)], ident[:, :])
                        at = 2 * HD + h * ROPE
                        mm = nc.tensor.transpose(banks[0:ROPE, 4 + t, tile_of(2 + h)],
                                                 turn_in[:, t, at:at + ROPE], ident[:, :])
                mm.then_inc(turned, 1)

            def turn_k2(j):
                pe.wait_ge(taken, 2 * (B_UKV + j) + 2)
                pe.wait_ge(kept, K_UKV + j)
                for t in range(TILES):
                    for h in range(2):
                        mm = nc.tensor.transpose(banks[:, 4 + t, tile_of(h)], turn_in[:, t, tile_of(h)], ident[:, :])
                mm.then_inc(turned, 1)

            def latent_up():
                width = 2 * (HD + ROPE)
                for j in range(UQ_BLOCKS):
                    pc = piece(UQ + j)
                    rhs = [cut(w, pc.split, QC, width) for w in (w_hi, w_lo)]
                    latent_block(pc, B_UQ + j, 0, QC, rhs, width).then_inc(piece_used, 1)
                    if j >= 1:
                        turn_q2(j - 1)
                for j in range(UKV_BLOCKS):
                    pc = piece(UKV + j // 2)
                    rhs = [cut(w, pc.split, KVC, 2 * BANK)[:, :, quarter(j % 2)] for w in (w_hi, w_lo)]
                    mm = latent_block(pc, B_UKV + j, QC, KVC, rhs, BANK)
                    mm.then_inc(piece_used if j % 2 else kv_half, 1)
                    if j == 0:
                        turn_q2(UQ_BLOCKS - 1)
                    else:
                        turn_k2(j - 1)
                turn_k2(UKV_BLOCKS - 1)

            def scores(u):
                s = banks[:, u % 2, :]
                if u >= 2:
                    pe.wait_ge(peaked, u - 1)
                h = u % HEADS
                for t, at in ((0, slice(0, P)), (1, slice(P, 3 * P))):
                    keys = slice(0, (t + 1) * P)
                    if u < HEADS:
                        mm = nc.tensor.matmul(s[:, at], qkT[:, h, tile_of(t)], qkT[:, HEADS + h, keys],
                                              start=True, stop=True)
                    else:
                        nc.tensor.matmul(s[:, at], q2T[:, h, tile_of(t)], k2T[:, h, keys], start=True, stop=False)
                        mm = nc.tensor.matmul(s[:, at], q2pT[:, h, tile_of(t)], k2pT[:, keys], start=False, stop=True)
                mm.then_inc(scores_ready, 1)

            def turn_probs(u):
                a = u % 2
                pe.wait_ge(probs_ready, u + 1)
                if u >= 2:
                    pe.wait_ge(probs_kept, u - 1)
                for n in range(3):
                    mm = nc.tensor.transpose(banks[:, 2 + a, tile_of(n)], probs[:, a, tile_of(n)], ident[:, :])
                mm.then_inc(probs_turned, 1)

            def weigh_values(u):
                a, h = u % 2, u % HEADS
                values = v1 if u < HEADS else v2
                cols = slice(h * HD, (h + 1) * HD)
                pe.wait_ge(probs_kept, u + 1)
                if u >= 2:
                    pe.wait_ge(head_out, u - 1)
                nc.tensor.matmul(banks[:, 4 + a, 0:P], probsT[:, a, 0:P], values[:, 0, cols], start=True, stop=True)
                nc.tensor.matmul(banks[:, 4 + a, P:2 * P], probsT[:, a, P:2 * P], values[:, 0, cols],
                                 start=True, stop=False)
                nc.tensor.matmul(banks[:, 4 + a, P:2 * P], probsT[:, a, 2 * P:], values[:, 1, cols],
                                 start=False, stop=True).then_inc(head_ready, 1)

            def attention():
                pe.wait_ge(kept, K_GU2)
                pe.wait_ge(taken, 2 * B_OUT)
                for u in range(2 * HEADS + 2):
                    if u < 2 * HEADS:
                        scores(u)
                    if 1 <= u <= 2 * HEADS:
                        turn_probs(u - 1)
                    if u >= 2:
                        weigh_values(u - 2)

            def mix_out():
                first_block(OUT, B_OUT, 2)
                for n in range(1, OUT_BLOCKS):
                    for i in range(4):
                        if i == 0 and n >= 2:
                            pe.wait_ge(squared, 16 + 2 * (n - 1))
                            pe.wait_ge(y_scaled, 4 + 2 * (n - 1))
                        out_piece(piece(OUT + 4 * n + i), i, n)

            def out_piece(pc, i, n):
                pe.wait_ge(lo_ready, pc.index + 1)
                rhs_hi, rhs_lo = cut(w_hi, pc.split, 4, BANK), cut(w_lo, pc.split, 4, BANK)
                for j in range(4):
                    c = 4 * i + j
                    for t in range(TILES):
                        mm = three_passes(result(n, t), act_hi[:, c, tile_of(t)], act_lo[:, c, tile_of(t)],
                                          rhs_hi[:, j, :], rhs_lo[:, j, :], start=(c == 0), stop=(c == DC - 1))
                mm.then_inc(piece_used, 1)

            pe.wait_ge(consts_made, 1)
            pe.wait_ge(gains_landed, 16 * 7)
            nc.tensor.transpose(banks[:, 7, 256:256 + G_ROWS], gain_in[:, :], ident[0:G_ROWS, 0:G_ROWS])\
              .then_inc(gains_turned, 1)
            pe.wait_ge(gains_kept, 1)
            gate_up(GU1, 0)
            down(GU1, DOWN1)
            mix_in()
            latent_up()
            attention()
            mix_out()
            gate_up(GU2, 3)
            down(GU2, DOWN2)


def rope_tables():
    parts = []
    for dim in (HD, ROPE):
        inv = (np.float32(1.0) / (np.float32(10000.0) ** (np.arange(0, dim, 2, dtype=np.float32) / np.float32(dim))))
        ang = np.arange(TOKENS, dtype=np.float32)[:, None] * inv.astype(np.float32)[None, :]
        parts += [np.cos(ang), -np.sin(ang), np.sin(ang)]
    return np.concatenate(parts, axis=1).astype(np.float32)


NAMES = ["x", "ffn1_pre_g", "ffn1_w_gate", "ffn1_w_up", "ffn1_w_down", "ffn1_post_g", "mix_pre_g", "w_in",
         "mla_q_norm_g", "mla_kv_norm_g", "mla_w_uq", "mla_w_ukv", "mla_out_g", "moba_out_g", "w_out",
         "mix_post_g", "ffn2_pre_g", "ffn2_w_gate", "ffn2_w_up", "ffn2_w_down", "ffn2_post_g"]


def kernel(**inputs):
    import concourse.bacc as bacc
    from concourse.bass_utils import run_bass_kernel_spmd

    nc = bacc.Bacc("TRN2", target_bir_lowering=False, num_devices=1)
    arrays, args = {}, []
    for name in NAMES:
        a = np.ascontiguousarray(inputs[name])
        arrays[f"in_{name}"] = a
        args.append(nc.dram_tensor(f"in_{name}", a.shape, mybir.dt.from_np(a.dtype), kind="ExternalInput").ap())
    table = rope_tables()
    arrays["in_rope"] = table
    args.append(nc.dram_tensor("in_rope", table.shape, F32, kind="ExternalInput").ap())
    shape = (1, TOKENS, D)
    args.append(nc.dram_tensor("out_rows", shape, F32, kind="ExternalOutput").ap())
    build_layer(nc, *args)
    return run_bass_kernel_spmd(nc, [arrays], core_ids=[0]).results[0]["out_rows"]
```

```python
from collections import namedtuple
from contextlib import ExitStack

import numpy as np

import concourse.bass as bass
from concourse import mybir

P = 128
TILES = 2
TOKENS = P * TILES
D = 2048
DC = D // P
FFN = 5632
FB = 256
N_FB = FFN // FB
FC = FFN // P
HEADS = 8
HD = 128
ROPE = 64
Q_RANK, KV_RANK = 512, 256
QC, KVC = Q_RANK // P, KV_RANK // P
BANK = 512
RAW = 4
PIECE = 2048
EPS = 1e-6
MASKED = -1e30
MOBA_SCALE = float(HD) ** -0.5
MLA_SCALE = float(HD + ROPE) ** -0.5

IN_BLOCKS, UQ_BLOCKS, UKV_BLOCKS, OUT_BLOCKS = 8, 4, 4, 4
LAT = KV_RANK + ROPE
UQ_WIDTH = 2 * (HD + ROPE)
GU1 = 0
DOWN1 = GU1 + 4 * N_FB
IN = DOWN1 + FC
UQ = IN + 4 * IN_BLOCKS
UKV = UQ + UQ_BLOCKS
OUT = UKV + UKV_BLOCKS // 2
GU2 = OUT + 4 * OUT_BLOCKS
DOWN2 = GU2 + 4 * N_FB
PIECES = DOWN2 + FC
HALF = FC // 2

B_GU1 = 0
B_IN = B_GU1 + N_FB
B_UQ = B_IN + IN_BLOCKS
B_UKV = B_UQ + UQ_BLOCKS
B_OUT = B_UKV + UKV_BLOCKS
B_GU2 = B_OUT

T_GU1 = 0
T_CKV = T_GU1 + N_FB
T_CQ = T_CKV + 1
T_QK = T_CQ + 1
T_UQ = T_QK + 4
T_UKV = T_UQ + UQ_BLOCKS
T_GU2 = T_UKV + UKV_BLOCKS

K_GU1 = T_GU1
K_QK, K_UQ, K_UKV, K_GU2 = T_QK - 1, T_UQ - 1, T_UKV - 1, T_GU2 - 1

G_Q, G_KV = 4 * DC, 4 * DC + QC
G_ROWS = 4 * DC + QC + KVC

MOBA_TAB, MLA_TAB = 3 * HD // 2, 3 * ROPE // 2

(R_PRE1, R_POST1, R_PRE_MIX, R_KV, R_Q, R_MOBA, R_MLA, R_POST_MIX, R_PRE2, R_POST2) = range(10)

ALU = mybir.AluOpType
ACT = mybir.ActivationFunctionType
F32 = mybir.dt.float32
F32R = mybir.dt.float32r
BF16 = mybir.dt.bfloat16

Piece = namedtuple("Piece", "index slot fills split")


def piece(first, i=0, step=0):
    return Piece(first + step * i, first % RAW, first // RAW + (step // RAW) * i, first % 2)


def build_layer(nc, x, xT_in, stream, gains, post_gains, rope, out):
    ctx = ExitStack()
    with ctx:
        def sb(name, shape, dt=F32, stack=ctx):
            return stack.enter_context(nc.sbuf_tensor(name, shape, dt))

        def sem(name):
            return ctx.enter_context(nc.semaphore(name))

        rows = sb("rows", [P, TILES, D])
        raw = sb("raw", [P, RAW, PIECE])
        w_hi = sb("w_hi", [P, 2, PIECE], F32R)
        w_lo = sb("w_lo", [P, 2, PIECE], F32R)
        gain_row = sb("gain_row", [P, D])
        ident = sb("ident", [P, P])
        mask = sb("mask", [P, 2 * P])
        gain_in = sb("gain_in", [G_ROWS, P])
        gain = sb("gain", [P, G_ROWS])
        tab = sb("tab", [P, TILES, MOBA_TAB + MLA_TAB])
        probs = sb("probs", [P, 2, 3 * P])
        sumsq = sb("sumsq", [P, TILES, 4])
        var = sb("var", [P, 10, TILES])
        rs = sb("rs", [P, 10, TILES])
        minus_half = sb("minus_half", [P, TILES])
        peak = sb("peak", [P, 2, TILES])
        shift = sb("shift", [P, 2, TILES])
        total = sb("total", [P, 2, TILES])
        rtotal = sb("rtotal", [P, 2, TILES])

        with ExitStack() as s:
            act_hi = sb("act_hi", [P, DC, TOKENS], F32R, s)
            act_lo = sb("act_lo", [P, DC, TOKENS], F32R, s)
        q2T = sb("q2T", [P, HEADS, TOKENS])
        k2T = sb("k2T", [P, HEADS, TOKENS])
        q2pT = sb("q2pT", [ROPE, HEADS, TOKENS])
        v2 = sb("v2", [P, TILES, HEADS * HD])

        with ExitStack() as s:
            hidT = sb("hidT", [P, FC, TOKENS], F32, s)
        qkT = sb("qkT", [P, 2 * HEADS, TOKENS])
        v1 = sb("v1", [P, TILES, HEADS * HD])
        heads = sb("heads", [P, TILES, D])
        k2pT = sb("k2pT", [ROPE, TOKENS])
        tab_r = sb("tab_r", [P, TILES, MOBA_TAB])
        tab_q = sb("tab_q", [P, TILES, MLA_TAB])
        sb("hid_pad", [P, 192])

        with ExitStack() as s:
            hid_split = sb("hid_split", [P, 2, 2, 2, TOKENS], F32R, s)
            silu = sb("silu", [P, TILES, FB], F32, s)
            hid = sb("hid", [P, TILES, FB], F32, s)
        with ExitStack() as s:
            sb("junk_at", [P, 2, 2, 2, TOKENS], F32, s)
            junk = sb("junk", [P, D], BF16, s)
        lat_hi = sb("lat_hi", [P, QC + KVC, TOKENS], F32R)
        lat_lo = sb("lat_lo", [P, QC + KVC, TOKENS], F32R)

        with ExitStack() as s:
            xT = sb("xT", [P, DC, TOKENS], F32, s)
        with ExitStack() as s:
            scaled = sb("scaled", [P, TILES, D], F32, s)
        with ExitStack() as s:
            lat = sb("lat", [P, TILES, Q_RANK + KV_RANK + ROPE], F32, s)
        masked = sb("masked", [P, 2, 3 * P])
        probsT = sb("probsT", [P, 2, 3 * P])
        sb("lat_pad", [P, 128])
        turn_in = sb("turn_in", [P, TILES, BANK])
        rot_a = sb("rot_a", [P, BANK])
        rot_b = sb("rot_b", [P, BANK])
        sb("scaled_pad", [P, 384])
        junk_mix = probs[:, 0, 0:256].bitcast(BF16)

        banks = ctx.enter_context(nc.psum_tensor("banks", [P, 8, BANK], F32))

        xT_landed = [sem(f"xT_landed{k}") for k in range(4)]
        rows_landed = sem("rows_landed")
        gains_landed = sem("gains_landed")
        tab_landed = sem("tab_landed")
        gain_row_landed = sem("gain_row_landed")
        raw_landed = [sem(f"raw_landed{s}") for s in range(RAW)]
        stored = sem("stored")
        zeroed = sem("zeroed")
        consts_made = sem("consts_made")
        gains_turned = sem("gains_turned")
        gains_kept = sem("gains_kept")
        hi_ready = sem("hi_ready")
        lo_ready = sem("lo_ready")
        hid_hi_ready = sem("hid_hi_ready")
        piece_used = sem("piece_used")
        tile0_done = sem("tile0_done")
        rows_ready = sem("rows_ready")
        quad_turned = sem("quad_turned")
        act_hi_ready = sem("act_hi_ready")
        act_ready = sem("act_ready")
        squared = sem("squared")
        var_ready = sem("var_ready")
        rs_ready = sem("rs_ready")
        silu_ready = sem("silu_ready")
        taken = sem("taken")
        turned = sem("turned")
        kept = sem("kept")
        tab_scaled = sem("tab_scaled")
        rot_step = sem("rot_step")
        pe_rows = sem("pe_rows")
        lat_hi_ready = sem("lat_hi_ready")
        lat_ready = sem("lat_ready")
        kv_half = sem("kv_half")
        y_scaled = sem("y_scaled")
        scores_ready = sem("scores_ready")
        peaked = sem("peaked")
        shifted = sem("shifted")
        probs_ready = sem("probs_ready")
        probs_turned = sem("probs_turned")
        probs_kept = sem("probs_kept")
        head_ready = sem("head_ready")
        totalled = sem("totalled")
        head_out = sem("head_out")

        x_dram = x.rearrange("b (t p) d -> p (b t) d", p=P)
        out_dram = out.rearrange("b (t p) d -> p (b t) d", p=P)

        def cut(t, slot, chunks, width):
            return t[:, slot, 0:chunks * width].rearrange("p (c n) -> p c n", c=chunks)

        def result(block, t):
            return banks[:, 2 * (block % 2) + t, :]

        def tile_of(t):
            return slice(t * P, (t + 1) * P)

        def quarter(k):
            return slice(k * BANK, (k + 1) * BANK)

        def down_banks(half, t):
            return ((6, 0), (2, 4))[half][t]

        def turn_bank(k, j):
            return (6, 4)[k % 2] + j // 2

        def turn_at(k, j):
            return banks[:, turn_bank(k, j), (j % 2) * TOKENS:(j % 2 + 1) * TOKENS]

        def turned_chunk(turn, c):
            return xT[:, c, :] if turn == 0 else turn_at(c // 4, c % 4)

        block = ctx.enter_context(nc.Block())

        @block.sync
        def _(sp):
            def raw_free(pc):
                if not (isinstance(pc.index, int) and pc.index < RAW):
                    sp.wait_ge(lo_ready, pc.index - RAW + 1)

            def load(pc, width=PIECE):
                raw_free(pc)
                sp.dma_start(raw[:, pc.slot, 0:width], stream[:, bass.ds(pc.index, 1), 0:width]
                             .rearrange("p o n -> p (o n)")).then_inc(raw_landed[pc.slot], 16)

            def load_from(first, end):
                with sp.Fori(0, (end - first) // RAW) as i:
                    for n in range(RAW):
                        load(piece(first + n, i, RAW))

            def load_gain_row(n, uses):
                sp.wait_ge(y_scaled, uses)
                sp.dma_start(gain_row[:, :], post_gains[n, :].partition_broadcast(P)).then_inc(gain_row_landed, 16)

            for n in range(RAW):
                load(piece(n))
                sp.dma_start(xT[:, 4 * n:4 * n + 4, :], xT_in[:, 4 * n:4 * n + 4, :]).then_inc(xT_landed[n], 16)
            sp.dma_start(rows[:, :, :], x_dram).then_inc(rows_landed, 16)
            load_from(RAW, IN)
            for n in range(4):
                load(piece(IN + n), 4 * LAT)
            load_from(IN + 4, IN + 12)
            load_gain_row(1, 4)
            load_from(IN + 12, UQ)
            for n in range(UQ_BLOCKS):
                load(piece(UQ + n), QC * UQ_WIDTH)
            load(piece(UKV))
            load(piece(UKV + 1))
            load_from(OUT, GU2 + 4)
            load_gain_row(2, 4 + 2 * OUT_BLOCKS)
            load_from(GU2 + 4, PIECES)
            for k in range(4):
                for t in range(TILES):
                    sp.wait_ge(rows_ready, 24 + 2 * k + t + 1)
                    sp.dma_start(out_dram[:, t, quarter(k)], rows[:, t, quarter(k)]).then_inc(stored, 16)
            sp.wait_ge(stored, 16 * 4 * TILES)

        @block.gpsimd
        def _(pool):
            nc.gpsimd.memset(ident[:, :], 0.0)
            nc.gpsimd.memset(mask[:, :], 0.0)
            nc.gpsimd.memset(minus_half[:, :], -0.5).then_inc(zeroed, 1)
            pool.wait_ge(zeroed, 1)
            nc.gpsimd.affine_select(out=ident[:, :], in_=ident[:, :], compare_op=ALU.not_equal, fill=1.0,
                                    base=0, pattern=[[-1, P]], channel_multiplier=1)
            nc.gpsimd.affine_select(out=mask[:, P:2 * P], in_=mask[:, P:2 * P], compare_op=ALU.is_ge,
                                    fill=MASKED, base=0, pattern=[[-1, P]], channel_multiplier=1)\
              .then_inc(consts_made, 1)

            steps = [0]

            def inverse_rms(job, sums, parts, width, factor, col=0):
                pool.wait_ge(squared, sums)
                for n in range(1, parts):
                    nc.gpsimd.tensor_tensor(sumsq[:, :, 0], sumsq[:, :, 0], sumsq[:, :, n], ALU.add)\
                      .then_inc(var_ready, 1)
                    steps[0] += 1
                    pool.wait_ge(var_ready, steps[0])
                c = factor ** -2
                nc.gpsimd.tensor_scalar(var[:, job, :], sumsq[:, :, col], c / width, c * EPS, ALU.mult, ALU.add)\
                  .then_inc(var_ready, 1)
                steps[0] += 1
                pool.wait_ge(var_ready, steps[0])
                nc.gpsimd.tensor_tensor(rs[:, job, :], var[:, job, :], minus_half[:, :], ALU.pow)\
                  .then_inc(rs_ready, 1)

            inverse_rms(R_PRE1, 2, 1, D, 1.0)
            inverse_rms(R_POST1, 6, 2, D, 0.5)
            inverse_rms(R_PRE_MIX, 8, 1, D, 1.0)
            inverse_rms(R_KV, 10, 1, KV_RANK, 1.0, col=2)
            inverse_rms(R_Q, 12, 1, Q_RANK, 1.0, col=3)
            inverse_rms(R_MOBA, 14, 1, HEADS * HD, 1.0, col=0)
            inverse_rms(R_MLA, 16, 1, HEADS * HD, 1.0, col=1)
            inverse_rms(R_POST_MIX, 24, 4, D, 1.0)
            inverse_rms(R_PRE2, 26, 1, D, 1.0)
            inverse_rms(R_POST2, 30, 2, D, 0.5)

        @block.scalar
        def _(act):
            def take_high(pc, width=PIECE):
                act.wait_ge(raw_landed[pc.slot], 16 * (pc.fills + 1))
                if not (isinstance(pc.index, int) and pc.index < 2):
                    act.wait_ge(piece_used, pc.index - 1)
                nc.scalar.activation(w_hi[:, pc.split, 0:width], raw[:, pc.slot, 0:width], ACT.Copy)\
                  .then_inc(hi_ready, 1)

            def turn_high(turn, k):
                if turn == 0:
                    act.wait_ge(xT_landed[k], 16)
                else:
                    act.wait_ge(quad_turned, 4 * (turn - 1) + k + 1)
                for j in range(4):
                    c = 4 * k + j
                    nc.scalar.activation(act_hi[:, c, :], turned_chunk(turn, c), ACT.Copy,
                                         scale=gain[:, DC * turn + c:DC * turn + c + 1]).then_inc(act_hi_ready, 1)

            squares = [0]

            def square(of, scratch, tile, col):
                if squares[0]:
                    act.wait_ge(squared, squares[0])
                nc.scalar.activation(scratch, of, ACT.Square, accum_out=sumsq[:, tile, col:col + 1])\
                  .then_inc(squared, 1)
                squares[0] += 1

            def square_rows():
                for t in range(TILES):
                    square(rows[:, t, :], junk[:, :], t, 0)

            def silu_block(stage, b):
                first = B_GU1 if stage == GU1 else B_GU2
                if not (isinstance(b, int) and b == 0):
                    act.wait_ge(taken, 2 * first + 2 * b)
                job = R_PRE1 if stage == GU1 else R_PRE2
                return first, job

            def gate(stage, b, parity):
                first, job = silu_block(stage, b)
                for t in range(TILES):
                    nc.scalar.activation(silu[:, t, :], result(parity, t)[:, 0:FB], ACT.Silu,
                                         scale=rs[:, job, t:t + 1]).then_inc(silu_ready, 1)

            def keep_hidden(stage, b):
                first = T_GU1 if stage == GU1 else T_GU2
                act.wait_ge(turned, first + b + 1)
                nc.scalar.copy(hidT[:, bass.ds(2 * b, 2), :],
                               banks[:, 4, :].rearrange("p (c n) -> p c n", c=2)).then_inc(kept, 1)

            def gate_up(stage, turn):
                if turn == 0:
                    take_high(piece(stage))
                turn_high(turn, 0)
                if turn == 0:
                    take_high(piece(stage + 1))
                turn_high(turn, 1)
                take_high(piece(stage + 2))
                turn_high(turn, 2)
                turn_high(turn, 3)
                act.wait_ge(rows_landed, 16)
                square_rows()
                take_high(piece(stage + 3))
                act.wait_ge(rs_ready, (R_PRE1 if stage == GU1 else R_PRE2) + 1)
                take_high(piece(stage + 4))
                take_high(piece(stage + 5))
                gate(stage, 0, 0)
                take_high(piece(stage + 6))
                take_high(piece(stage + 7))
                keep_hidden(stage, 0)
                with act.Fori(0, (N_FB - 2) // 2) as n:
                    for e in range(2):
                        for i in range(4):
                            take_high(piece(stage + 8 + 4 * e + i, n, 8))
                            if i == 1:
                                gate(stage, 2 * n + (e + 1), (e + 1) % 2)
                        keep_hidden(stage, 2 * n + (e + 1))

            def take_high_down(pc, n):
                act.wait_ge(raw_landed[pc.slot], 16 * (pc.fills + 1))
                act.wait_ge(piece_used, pc.index - 1)
                nc.scalar.activation(w_hi[:, pc.split, :], raw[:, pc.slot, :], ACT.Copy).then_inc(hi_ready, 1)
                nc.scalar.copy(hid_split[:, pc.split, 0], hidT[:, bass.ds(2 * n, 2), :]).then_inc(hid_hi_ready, 1)

            def square_down(stage, half):
                done = (half + 1) * HALF
                for t in range(TILES):
                    if t == 0:
                        act.wait_ge(tile0_done, done + (FC + OUT_BLOCKS if stage == DOWN2 else 0))
                    else:
                        act.wait_ge(piece_used, stage + done)
                    b = down_banks(half, t)
                    square(banks[:, b:b + 2, :].rearrange("p b n -> p (b n)"), junk[:, 0:D // 2], t, half)

            def down(gu_stage, stage):
                take_high_down(piece(stage), 0)
                take_high_down(piece(stage + 1), 1)
                gate(gu_stage, N_FB - 1, 1)
                keep_hidden(gu_stage, N_FB - 1)
                with act.Fori(0, (HALF - 2) // 4) as i:
                    for n in range(2, 6):
                        take_high_down(piece(stage + n, i, 4), 4 * i + n)
                take_high_down(piece(stage + HALF), 0)
                take_high_down(piece(stage + HALF + 1), 1)
                square_down(stage, 0)
                with act.Fori(0, (HALF - 2) // 4) as i:
                    for n in range(2, 6):
                        take_high_down(piece(stage + HALF + n, i, 4), 4 * i + n)

            def keep_qk(j):
                act.wait_ge(turned, T_QK + 1 + j)
                for t in range(TILES):
                    ins = nc.scalar.copy(qkT[:, bass.ds(4 * j, 4), tile_of(t)],
                                         banks[:, 4 + t, :].rearrange("p (h n) -> p h n", h=4))
                ins.then_inc(kept, 1)

            def latent_high(first, chunks, bank, g):
                for c in range(chunks):
                    nc.scalar.activation(lat_hi[:, first + c, :],
                                         banks[:, bank + c // 2, (c % 2) * TOKENS:(c % 2 + 1) * TOKENS],
                                         ACT.Copy, scale=gain[:, g + c:g + c + 1]).then_inc(lat_hi_ready, 1)

            def square_latent(tiles_taken, cols, col):
                act.wait_ge(taken, tiles_taken)
                for t in range(TILES):
                    square(lat[:, t, cols], junk_mix[:, 0:cols.stop - cols.start], t, col)

            def keep_q2(j):
                act.wait_ge(turned, T_UQ + j + 1)
                for t in range(TILES):
                    b = banks[:, 4 + t, :].rearrange("p (h n) -> p h n", h=4)
                    nc.scalar.copy(q2T[:, 2 * j:2 * j + 2, tile_of(t)], b[:, 0:2, :])
                    ins = nc.scalar.copy(q2pT[:, 2 * j:2 * j + 2, tile_of(t)], b[0:ROPE, 2:4, :])
                ins.then_inc(kept, 1)

            def keep_k2(j):
                act.wait_ge(turned, T_UKV + j + 1)
                for t in range(TILES):
                    b = banks[:, 4 + t, :].rearrange("p (h n) -> p h n", h=4)
                    ins = nc.scalar.copy(k2T[:, 2 * j:2 * j + 2, tile_of(t)], b[:, 0:2, :])
                ins.then_inc(kept, 1)

            def mix_in():
                turn_high(1, 0)
                turn_high(1, 1)
                take_high(piece(IN + 2), 4 * LAT)
                turn_high(1, 2)
                turn_high(1, 3)
                square_rows()
                take_high(piece(IN + 3), 4 * LAT)
                take_high(piece(IN + 4))
                take_high(piece(IN + 5))
                square_latent(2 * B_IN + 2, slice(Q_RANK, Q_RANK + KV_RANK), 2)
                take_high(piece(IN + 6))
                take_high(piece(IN + 7))
                act.wait_ge(turned, T_CKV + 1)
                latent_high(QC, KVC, 6, G_KV)
                nc.scalar.copy(k2pT[:, :], banks[0:ROPE, 7, 0:TOKENS]).then_inc(kept, 1)
                take_high(piece(IN + 8))
                take_high(piece(IN + 9))
                square_latent(2 * B_IN + 4, slice(0, Q_RANK), 3)
                take_high(piece(IN + 10))
                take_high(piece(IN + 11))
                act.wait_ge(turned, T_CQ + 1)
                latent_high(0, QC, 4, G_Q)
                with act.Fori(0, 2) as n:
                    for e in range(2):
                        for i in range(4):
                            take_high(piece(IN + 12 + 4 * e + i, n, 8))
                        keep_qk(2 * n + e)
                for i in range(4):
                    take_high(piece(IN + 28 + i))

            def latent_up():
                uq_width = QC * 2 * (HD + ROPE)
                take_high(piece(UQ), uq_width)
                take_high(piece(UQ + 1), uq_width)
                take_high(piece(UQ + 2), uq_width)
                keep_q2(0)
                take_high(piece(UQ + 3), uq_width)
                keep_q2(1)
                take_high(piece(UKV))
                keep_q2(2)
                take_high(piece(UKV + 1))
                keep_q2(3)
                keep_k2(0)
                take_high(piece(OUT))
                keep_k2(1)
                keep_k2(2)
                take_high(piece(OUT + 1))
                keep_k2(3)

            def attention():
                for u in range(2 * HEADS + 1):
                    if u < 2 * HEADS:
                        a = u % 2
                        scale = MOBA_SCALE if u < HEADS else MLA_SCALE
                        act.wait_ge(shifted, u + 1)
                        if u >= 2:
                            act.wait_ge(probs_turned, u - 1)
                            act.wait_ge(totalled, u - 1)
                        nc.scalar.activation(probs[:, a, 0:P], masked[:, a, 0:P], ACT.Exp, bias=shift[:, a, 0:1],
                                             scale=scale, accum_out=total[:, a, 0:1])
                        nc.scalar.activation(probs[:, a, P:], masked[:, a, P:], ACT.Exp, bias=shift[:, a, 1:2],
                                             scale=scale, accum_out=total[:, a, 1:2]).then_inc(probs_ready, 1)
                    if u >= 1:
                        a = (u - 1) % 2
                        act.wait_ge(probs_turned, u)
                        if u >= 3:
                            act.wait_ge(head_ready, u - 2)
                        nc.scalar.copy(probsT[:, a, :], banks[:, 2 + a, 0:3 * P]).then_inc(probs_kept, 1)
                    if u == HEADS + 3:
                        square_heads(1, HEADS)
                square_heads(0, 2 * HEADS)

            def square_heads(half, done):
                act.wait_ge(head_out, done)
                for t in range(TILES):
                    square(heads[:, t, half * D // 2:(half + 1) * D // 2], rot_a[:, :].bitcast(BF16), t, 1 - half)

            def square_out(n):
                for t in range(TILES):
                    if t == 0:
                        act.wait_ge(tile0_done, FC + n + 1)
                    else:
                        act.wait_ge(piece_used, OUT + 4 * n + 4)
                    square(result(n, t), junk[:, 0:BANK], t, n)

            def mix_out():
                turn_high(2, 0)
                turn_high(2, 1)
                take_high(piece(OUT + 2))
                turn_high(2, 2)
                turn_high(2, 3)
                take_high(piece(OUT + 3))
                for n in range(1, OUT_BLOCKS):
                    take_high(piece(OUT + 4 * n))
                    take_high(piece(OUT + 4 * n + 1))
                    square_out(n - 1)
                    take_high(piece(OUT + 4 * n + 2))
                    take_high(piece(OUT + 4 * n + 3))
                take_high(piece(GU2))
                square_out(OUT_BLOCKS - 1)
                take_high(piece(GU2 + 1))

            act.dma_start(gain_in[:, :], gains).then_inc(gains_landed, 16)
            act.dma_start(tab[:, :, :], rope.rearrange("(t p) n -> p t n", p=P)).then_inc(tab_landed, 16)
            act.dma_start(gain_row[:, :], post_gains[0, :].partition_broadcast(P)).then_inc(gain_row_landed, 16)
            act.wait_ge(gains_turned, 1)
            nc.scalar.copy(gain[:, :], banks[:, 7, 256:256 + G_ROWS]).then_inc(gains_kept, 1)
            act.wait_ge(gains_kept, 1)

            gate_up(GU1, 0)
            down(GU1, DOWN1)
            take_high(piece(IN), 4 * LAT)
            square_down(DOWN1, 1)
            take_high(piece(IN + 1), 4 * LAT)
            mix_in()
            latent_up()
            attention()
            mix_out()
            gate_up(GU2, 3)
            down(GU2, DOWN2)
            square_down(DOWN2, 1)

        @block.vector
        def _(dve):
            def take_low(pc, width=PIECE):
                dve.wait_ge(hi_ready, pc.index + 1)
                nc.vector.tensor_tensor(w_lo[:, pc.split, 0:width], raw[:, pc.slot, 0:width],
                                        w_hi[:, pc.split, 0:width], ALU.subtract).then_inc(lo_ready, 1)

            def turn_low(turn, k):
                for j in range(4):
                    c = 4 * k + j
                    if j % 2 == 0:
                        dve.wait_ge(act_hi_ready, DC * turn + c + 2)
                    nc.vector.scalar_tensor_tensor(
                        out=act_lo[:, c, :], in0=turned_chunk(turn, c), scalar=gain[:, DC * turn + c:DC * turn + c + 1],
                        in1=act_hi[:, c, :], op0=ALU.mult, op1=ALU.subtract).then_inc(act_ready, 1)

            def multiply_hidden(stage, b, parity):
                blocks, turns, job = ((B_GU1, T_GU1, R_PRE1) if stage == GU1 else (B_GU2, T_GU2, R_PRE2))
                if not (isinstance(b, int) and b == 0):
                    dve.wait_ge(turned, turns + b)
                for t in range(TILES):
                    dve.wait_ge(silu_ready, b * 2 + (2 * turns_before(stage) + t + 1))
                    nc.vector.scalar_tensor_tensor(
                        out=hid[:, t, :], in0=result(parity, t)[:, FB:], scalar=rs[:, job, t:t + 1],
                        in1=silu[:, t, :], op0=ALU.mult, op1=ALU.mult).then_inc(taken, 1)

            def turns_before(stage):
                return 0 if stage == GU1 else N_FB

            def add_residual(job, turn, second_piece=None):
                for k in range(4):
                    for t in range(TILES):
                        if k == 0 and t == 0:
                            dve.wait_ge(rs_ready, job + 1)
                            dve.wait_ge(y_scaled, scaled_parts[job])
                        nc.vector.scalar_tensor_tensor(
                            out=rows[:, t, quarter(k)], in0=scaled[:, t, quarter(k)], scalar=rs[:, job, t:t + 1],
                            in1=rows[:, t, quarter(k)], op0=ALU.mult, op1=ALU.add).then_inc(rows_ready, 1)
                    if turn is not None and k >= 1:
                        turn_low(turn, k - 1)
                    if turn is not None and k == 1:
                        take_low(*second_piece)
                if turn is not None:
                    turn_low(turn, 3)

            scaled_parts = {R_POST1: 4, R_POST_MIX: 4 + 2 * OUT_BLOCKS, R_POST2: 8 + 2 * OUT_BLOCKS}

            def gate_up(stage):
                for i in range(2, 4):
                    take_low(piece(stage + i))
                dve.wait_ge(rs_ready, (R_PRE1 if stage == GU1 else R_PRE2) + 1)
                take_low(piece(stage + 4))
                take_low(piece(stage + 5))
                multiply_hidden(stage, 0, 0)
                take_low(piece(stage + 6))
                take_low(piece(stage + 7))
                with dve.Fori(0, (N_FB - 2) // 2) as n:
                    for e in range(2):
                        for i in range(4):
                            take_low(piece(stage + 8 + 4 * e + i, n, 8))
                            if i == 1:
                                multiply_hidden(stage, 2 * n + (e + 1), (e + 1) % 2)

            def take_low_down(pc, n, hid_base):
                dve.wait_ge(hi_ready, pc.index + 1)
                nc.vector.tensor_tensor(w_lo[:, pc.split, :], raw[:, pc.slot, :], w_hi[:, pc.split, :],
                                        ALU.subtract)
                dve.wait_ge(hid_hi_ready, pc.index - hid_base + 1)
                nc.vector.tensor_tensor(hid_split[:, pc.split, 1], hidT[:, bass.ds(2 * n, 2), :],
                                        hid_split[:, pc.split, 0], ALU.subtract).then_inc(lo_ready, 1)

            def scale_down(half, sums_before):
                cols = slice(half * D // 2, (half + 1) * D // 2)
                for t in range(TILES):
                    dve.wait_ge(squared, sums_before + t + 1)
                    b = down_banks(half, t)
                    nc.vector.tensor_tensor(scaled[:, t, cols], banks[:, b:b + 2, :].rearrange("p b n -> p (b n)"),
                                            gain_row[:, cols], ALU.mult).then_inc(y_scaled, 1)

            def down(gu_stage, stage, sums_before, gain_loads):
                base = DOWN1 if stage == DOWN1 else DOWN2 - FC
                take_low_down(piece(stage), 0, base)
                take_low_down(piece(stage + 1), 1, base)
                multiply_hidden(gu_stage, N_FB - 1, 1)
                with dve.Fori(0, (HALF - 2) // 4) as i:
                    for n in range(2, 6):
                        take_low_down(piece(stage + n, i, 4), 4 * i + n, base)
                take_low_down(piece(stage + HALF), 0, base)
                take_low_down(piece(stage + HALF + 1), 1, base)
                dve.wait_ge(gain_row_landed, 16 * gain_loads)
                scale_down(0, sums_before)
                with dve.Fori(0, (HALF - 2) // 4) as i:
                    for n in range(2, 6):
                        take_low_down(piece(stage + HALF + n, i, 4), 4 * i + n, base)

            def rotate(to, of, table, n_heads, half, wait_first=True):
                def by_head(ap):
                    return ap.rearrange("p (h a d) -> p h a d", h=n_heads, a=2)
                n = n_heads * 2 * half
                a, b = by_head(rot_a[:, 0:n]), by_head(rot_b[:, 0:n])

                def bc(lo, reps):
                    shape = [P, n_heads] + reps + [half]
                    t = table[:, lo:lo + half].unsqueeze(1)
                    if reps:
                        t = t.unsqueeze(1)
                    return t.to_broadcast(shape)
                nc.vector.tensor_tensor(a, of, bc(0, [2]), ALU.mult)
                nc.vector.tensor_tensor(b[:, :, 0, :], of[:, :, 1, :], bc(half, []), ALU.mult)
                nc.vector.tensor_tensor(b[:, :, 1, :], of[:, :, 0, :], bc(2 * half, []), ALU.mult)\
                  .then_inc(rot_step, 1)
                return a, b, to

            def rotate_done(a, b, to, count):
                dve.wait_ge(rot_step, count)
                return nc.vector.tensor_tensor(to, a, b, ALU.add)

            def rotate_qk(j, parity):
                dve.wait_ge(piece_used, j * 4 + (IN + 4 * 3))
                dve.wait_ge(turned, T_QK + j)
                for t in range(TILES):
                    if t == 1:
                        dve.wait_ge(taken, j * 2 + (2 * (B_IN + 2) + 1))
                    of = result(parity, t).rearrange("p (h a d) -> p h a d", h=4, a=2)
                    to = turn_in[:, t, :].rearrange("p (h a d) -> p h a d", h=4, a=2)
                    a, b, to = rotate(to, of, tab_r[:, t, :], 4, HD // 2)
                    rotate_done(a, b, to, j * 2 + (2 + t + 1)).then_inc(taken, 1)

            def scale_latent(b, width, at):
                dve.wait_ge(piece_used, IN + 4 * (b + 1))
                for t in range(TILES):
                    nc.vector.tensor_scalar(lat[:, t, at:at + width], result(b, t)[:, 0:width],
                                            rs[:, R_PRE_MIX, t:t + 1], None, ALU.mult).then_inc(taken, 1)

            def latent_low(first, chunks, bank, g):
                for c in range(chunks):
                    if c % 2 == 0:
                        dve.wait_ge(lat_hi_ready, lat_order(first) + c + 2)
                    nc.vector.scalar_tensor_tensor(
                        out=lat_lo[:, first + c, :],
                        in0=banks[:, bank + c // 2, (c % 2) * TOKENS:(c % 2 + 1) * TOKENS],
                        scalar=gain[:, g + c:g + c + 1], in1=lat_hi[:, first + c, :],
                        op0=ALU.mult, op1=ALU.subtract).then_inc(lat_ready, 1)

            def lat_order(first):
                return 0 if first == QC else KVC

            def scale_v1(n, parity):
                dve.wait_ge(piece_used, IN + 4 * (7 + n))
                for t in range(TILES):
                    nc.vector.tensor_scalar(v1[:, t, quarter(n)], result(parity, t),
                                            rs[:, R_PRE_MIX, t:t + 1], None, ALU.mult).then_inc(taken, 1)

            def mix_in():
                for i in range(2, 4):
                    take_low(piece(IN + i), 4 * LAT)
                take_low(piece(IN + 4))
                take_low(piece(IN + 5))
                dve.wait_ge(rs_ready, R_PRE_MIX + 1)
                dve.wait_ge(tab_landed, 16)
                for t in range(TILES):
                    nc.vector.tensor_scalar(tab_r[:, t, :], tab[:, t, 0:MOBA_TAB], rs[:, R_PRE_MIX, t:t + 1],
                                            None, ALU.mult).then_inc(tab_scaled, 1)
                scale_latent(0, LAT, Q_RANK)
                dve.wait_ge(taken, 2 * B_IN + 2)
                for t in range(TILES):
                    at = Q_RANK + KV_RANK
                    if t == 1:
                        dve.wait_ge(pe_rows, 1)
                    of = lat[:, t, at:at + ROPE].rearrange("p (h a d) -> p h a d", h=1, a=2)
                    to = turn_in[:, t, 0:ROPE].rearrange("p (h a d) -> p h a d", h=1, a=2)
                    a, b, to = rotate(to, of, tab[:, t, MOBA_TAB:], 1, ROPE // 2)
                    rotate_done(a, b, to, t + 1).then_inc(pe_rows, 1)
                take_low(piece(IN + 6))
                take_low(piece(IN + 7))
                latent_low(QC, KVC, 6, G_KV)
                take_low(piece(IN + 8))
                take_low(piece(IN + 9))
                scale_latent(1, Q_RANK, 0)
                take_low(piece(IN + 10))
                take_low(piece(IN + 11))
                latent_low(0, QC, 4, G_Q)
                dve.wait_ge(tab_scaled, 2)
                with dve.Fori(0, 2) as n:
                    for e in range(2):
                        for i in range(4):
                            take_low(piece(IN + 12 + 4 * e + i, n, 8))
                            if i == 1:
                                rotate_qk(2 * n + e, e)
                take_low(piece(IN + 28))
                take_low(piece(IN + 29))
                scale_v1(0, 0)
                take_low(piece(IN + 30))
                take_low(piece(IN + 31))

            def split_q2(j):
                dve.wait_ge(piece_used, UQ + j + 1)
                dve.wait_ge(turned, T_UQ + j)
                for t in range(TILES):
                    if t == 1:
                        dve.wait_ge(taken, 2 * (B_UQ + j) + 1)
                    of = result(j, t)[:, 0:2 * (HD + ROPE)].rearrange("p (h n) -> p h n", h=2)
                    nc.vector.tensor_scalar(turn_in[:, t, 0:2 * HD].rearrange("p (h n) -> p h n", h=2),
                                            of[:, :, 0:HD], rs[:, R_Q, t:t + 1], None, ALU.mult)
                    to = turn_in[:, t, 2 * HD:2 * HD + 2 * ROPE].rearrange("p (h a d) -> p h a d", h=2, a=2)
                    a, b, to = rotate(to, of[:, :, HD:].rearrange("p h (a d) -> p h a d", a=2),
                                      tab_q[:, t, :], 2, ROPE // 2)
                    rotate_done(a, b, to, 10 + 2 * j + t + 1).then_inc(taken, 1)

            def split_kv2(j):
                dve.wait_ge(turned, T_UKV + j)
                if j % 2 == 0:
                    dve.wait_ge(kv_half, j // 2 + 1)
                else:
                    dve.wait_ge(piece_used, UKV + j // 2 + 1)
                for t in range(TILES):
                    of = result(j, t).rearrange("p (h n) -> p h n", h=2)
                    nc.vector.tensor_scalar(turn_in[:, t, 0:2 * HD].rearrange("p (h n) -> p h n", h=2),
                                            of[:, :, 0:HD], rs[:, R_KV, t:t + 1], None, ALU.mult)
                    nc.vector.tensor_scalar(v2[:, t, 2 * j * HD:(2 * j + 2) * HD].rearrange("p (h n) -> p h n", h=2),
                                            of[:, :, HD:], rs[:, R_KV, t:t + 1], None, ALU.mult).then_inc(taken, 1)

            def latent_up():
                uq_width = QC * 2 * (HD + ROPE)
                dve.wait_ge(rs_ready, R_Q + 1)
                for t in range(TILES):
                    nc.vector.tensor_scalar(tab_q[:, t, :], tab[:, t, MOBA_TAB:], rs[:, R_Q, t:t + 1],
                                            None, ALU.mult).then_inc(tab_scaled, 1)
                take_low(piece(UQ), uq_width)
                take_low(piece(UQ + 1), uq_width)
                scale_v1(1, 1)
                dve.wait_ge(tab_scaled, 4)
                split_q2(0)
                take_low(piece(UQ + 2), uq_width)
                split_q2(1)
                take_low(piece(UQ + 3), uq_width)
                split_q2(2)
                take_low(piece(UKV))
                split_q2(3)
                take_low(piece(UKV + 1))
                split_kv2(0)
                split_kv2(1)
                take_low(piece(OUT))
                split_kv2(2)
                split_kv2(3)
                take_low(piece(OUT + 1))

            def attention():
                for u in range(2 * HEADS + 2):
                    if u < 2 * HEADS:
                        a = u % 2
                        scale = MOBA_SCALE if u < HEADS else MLA_SCALE
                        s = banks[:, a, :]
                        dve.wait_ge(scores_ready, u + 1)
                        if u >= 2:
                            dve.wait_ge(probs_ready, u - 1)
                        nc.vector.tensor_tensor_reduce(
                            out=masked[:, a, 0:P], in0=s[:, 0:P], in1=mask[:, P:], scale=1.0, scalar=3 * MASKED,
                            op0=ALU.add, op1=ALU.max, accum_out=peak[:, a, 0:1])
                        nc.vector.tensor_tensor_reduce(
                            out=masked[:, a, P:], in0=s[:, P:3 * P], in1=mask[:, :], scale=1.0, scalar=3 * MASKED,
                            op0=ALU.add, op1=ALU.max, accum_out=peak[:, a, 1:2]).then_inc(peaked, 1)
                        dve.wait_ge(peaked, u + 1)
                        nc.vector.tensor_scalar(shift[:, a, :], peak[:, a, :], -scale, None, ALU.mult)\
                          .then_inc(shifted, 1)
                    if u >= 2:
                        v = u - 2
                        a = v % 2
                        at = (D // 2 if v < HEADS else 0) + (v % HEADS) * HD
                        dve.wait_ge(probs_ready, v + 1)
                        nc.vector.reciprocal(rtotal[:, a, :], total[:, a, :]).then_inc(totalled, 1)
                        dve.wait_ge(totalled, v + 1)
                        dve.wait_ge(head_ready, v + 1)
                        for t in range(TILES):
                            ins = nc.vector.tensor_scalar(heads[:, t, at:at + HD], banks[:, 4 + a, tile_of(t)],
                                                          rtotal[:, a, t:t + 1], None, ALU.mult)
                        ins.then_inc(head_out, 1)

            def mix_out():
                dve.wait_ge(rs_ready, R_MLA + 1)
                dve.wait_ge(head_out, 2 * HEADS)
                for k in range(4):
                    for t in range(TILES):
                        job = R_MLA if k < 2 else R_MOBA
                        nc.vector.tensor_scalar(heads[:, t, quarter(k)], heads[:, t, quarter(k)],
                                                rs[:, job, t:t + 1], None, ALU.mult).then_inc(rows_ready, 1)
                    if k >= 1:
                        turn_low(2, k - 1)
                turn_low(2, 3)
                take_low(piece(OUT + 2))
                take_low(piece(OUT + 3))
                dve.wait_ge(gain_row_landed, 32)
                for n in range(1, OUT_BLOCKS):
                    take_low(piece(OUT + 4 * n))
                    take_low(piece(OUT + 4 * n + 1))
                    scale_out(n - 1)
                    take_low(piece(OUT + 4 * n + 2))
                    take_low(piece(OUT + 4 * n + 3))
                take_low(piece(GU2))
                scale_out(OUT_BLOCKS - 1)

            def scale_out(n):
                for t in range(TILES):
                    dve.wait_ge(squared, 16 + 2 * n + t + 1)
                    nc.vector.tensor_tensor(scaled[:, t, quarter(n)], result(n, t), gain_row[:, quarter(n)],
                                            ALU.mult).then_inc(y_scaled, 1)

            dve.wait_ge(gains_kept, 1)
            take_low(piece(GU1))
            turn_low(0, 0)
            take_low(piece(GU1 + 1))
            turn_low(0, 1)
            turn_low(0, 2)
            turn_low(0, 3)
            gate_up(GU1)
            down(GU1, DOWN1, 2, 1)
            take_low(piece(IN), 4 * LAT)
            scale_down(1, 4)
            add_residual(R_POST1, 1, (piece(IN + 1), 4 * LAT))
            mix_in()
            latent_up()
            attention()
            mix_out()
            add_residual(R_POST_MIX, 3, (piece(GU2 + 1),))
            gate_up(GU2)
            down(GU2, DOWN2, 26, 3)
            scale_down(1, 28)
            add_residual(R_POST2, None)

        @block.tensor
        def _(pe):
            def three_passes(out_ap, hi, lo, rhs_hi, rhs_lo, start, stop, chain=False):
                nc.tensor.matmul(out_ap, hi, rhs_hi, start=start, stop=False, skip_group_check=chain)
                nc.tensor.matmul(out_ap, hi, rhs_lo, start=False, stop=False, skip_group_check=chain)
                return nc.tensor.matmul(out_ap, lo, rhs_hi, start=False, stop=stop, skip_group_check=chain)

            def turn(n_turn, k):
                source = heads if n_turn == 2 else rows
                if k >= 2:
                    pe.wait_ge(act_ready, DC * n_turn + 4 * (k - 1))
                for t in range(TILES):
                    pe.wait_ge(rows_ready, 8 * (n_turn - 1) + 2 * k + t + 1)
                    for j in range(4):
                        c = 4 * k + j
                        mm = nc.tensor.transpose(turn_at(k, j)[:, tile_of(t)],
                                                 source[:, t, c * P:(c + 1) * P], ident[:, :])
                mm.then_inc(quad_turned, 1)

            def dense_piece(pc, i, blk, parity, width=BANK, n_turn=None):
                pe.wait_ge(lo_ready, pc.index + 1)
                if i == 0 and not (isinstance(blk, int) and blk in (B_GU1, B_GU1 + 1)):
                    pe.wait_ge(taken, blk * 2 - 2)
                rhs_hi, rhs_lo = cut(w_hi, pc.split, 4, width), cut(w_lo, pc.split, 4, width)
                for j in range(4):
                    c = 4 * i + j
                    if n_turn is not None:
                        pe.wait_ge(act_ready, DC * n_turn + c + 1)
                    for t in range(TILES):
                        mm = three_passes(result(parity, t)[:, 0:width], act_hi[:, c, tile_of(t)],
                                          act_lo[:, c, tile_of(t)], rhs_hi[:, j, :], rhs_lo[:, j, :],
                                          start=(c == 0), stop=(c == DC - 1))
                mm.then_inc(piece_used, 1)

            def first_block(at, blk, n_turn, width=BANK):
                if n_turn:
                    turn(n_turn, 0)
                    turn(n_turn, 1)
                dense_piece(piece(at), 0, blk, 0, width, n_turn)
                if n_turn:
                    turn(n_turn, 2)
                    turn(n_turn, 3)
                dense_piece(piece(at + 1), 1, blk, 0, width, n_turn)
                dense_piece(piece(at + 2), 2, blk, 0, width, n_turn)
                dense_piece(piece(at + 3), 3, blk, 0, width, n_turn)

            def turn_hidden(stage, b):
                blocks, keeps = ((B_GU1, K_GU1) if stage == GU1 else (B_GU2, K_GU2))
                if not (isinstance(b, int) and b == 0):
                    pe.wait_ge(kept, keeps + b)
                pe.wait_ge(taken, b * 2 + (2 * blocks + 2))
                for c in range(2):
                    for t in range(TILES):
                        mm = nc.tensor.transpose(banks[:, 4, c * TOKENS + t * P:c * TOKENS + (t + 1) * P],
                                                 hid[:, t, tile_of(c)], ident[:, :])
                mm.then_inc(turned, 1)

            def gate_up(stage, n_turn):
                blocks = B_GU1 if stage == GU1 else B_GU2
                first_block(stage, blocks, n_turn)
                for i in range(4):
                    dense_piece(piece(stage + 4 + i), i, blocks + 1, 1)
                    if i == 1:
                        turn_hidden(stage, 0)
                with pe.Fori(0, (N_FB - 2) // 2) as n:
                    for e in range(2):
                        for i in range(4):
                            dense_piece(piece(stage + 8 + 4 * e + i, n, 8), i, n * 2 + (blocks + 2 + e), e)
                            if i == 1:
                                turn_hidden(stage, n * 2 + (1 + e))

            def down_piece(pc, half):
                pe.wait_ge(lo_ready, pc.index + 1)
                rhs_hi, rhs_lo = cut(w_hi, pc.split, 2, D // 2), cut(w_lo, pc.split, 2, D // 2)
                for t in range(TILES):
                    b = down_banks(half, t)
                    for j in range(2):
                        hi = hid_split[:, pc.split, 0, j, tile_of(t)]
                        lo = hid_split[:, pc.split, 1, j, tile_of(t)]
                        for lhs, rhs in ((hi, rhs_hi), (hi, rhs_lo), (lo, rhs_hi)):
                            for n in range(2):
                                mm = nc.tensor.matmul(banks[:, b + n, :], lhs, rhs[:, j, quarter(n)],
                                                      start=False, stop=True, skip_group_check=True)
                    mm.then_inc(piece_used if t else tile0_done, 1)

            def open_banks(half):
                for t in range(TILES):
                    for n in range(2):
                        nc.tensor.matmul(banks[:, down_banks(half, t) + n, 0:2], mask[:, 0:P], mask[:, 0:2],
                                         start=True, stop=True, skip_group_check=True)

            def down(gu_stage, stage):
                blocks, keeps = ((B_GU1, K_GU1) if gu_stage == GU1 else (B_GU2, K_GU2))
                pe.wait_ge(taken, 2 * blocks + 2 * (N_FB - 1))
                open_banks(0)
                down_piece(piece(stage), 0)
                turn_hidden(gu_stage, N_FB - 1)
                down_piece(piece(stage + 1), 0)
                with pe.Fori(0, (HALF - 2) // 4) as i:
                    for n in range(2, 6):
                        down_piece(piece(stage + n, i, 4), 0)
                pe.wait_ge(kept, keeps + N_FB)
                open_banks(1)
                for n in range(2):
                    down_piece(piece(stage + HALF + n), 1)
                with pe.Fori(0, (HALF - 2) // 4) as i:
                    for n in range(2, 6):
                        down_piece(piece(stage + HALF + n, i, 4), 1)

            def turn_latent(first, chunks, bank, col, count):
                pe.wait_ge(taken, count)
                for c in range(chunks):
                    for t in range(TILES):
                        mm = nc.tensor.transpose(banks[:, bank + c // 2, (c % 2) * TOKENS + t * P:
                                                       (c % 2) * TOKENS + (t + 1) * P],
                                                 lat[:, t, col + c * P:col + (c + 1) * P], ident[:, :])
                return mm

            def turn_qk(j):
                pe.wait_ge(taken, j * 2 + (2 * (B_IN + 2) + 2))
                pe.wait_ge(kept, K_QK + j)
                for t in range(TILES):
                    for h in range(4):
                        mm = nc.tensor.transpose(banks[:, 4 + t, tile_of(h)], turn_in[:, t, tile_of(h)], ident[:, :])
                mm.then_inc(turned, 1)

            def mix_in():
                first_block(IN, B_IN, 1, LAT)
                for i in range(4):
                    dense_piece(piece(IN + 4 + i), i, B_IN + 1, 1)
                    if i == 1:
                        pe.wait_ge(act_ready, 2 * DC)
                        turn_latent(QC, KVC, 6, Q_RANK, 2 * B_IN + 2)
                        pe.wait_ge(pe_rows, 2)
                        for t in range(TILES):
                            mm = nc.tensor.transpose(banks[0:ROPE, 7, tile_of(t)], turn_in[:, t, 0:ROPE], ident[:, :])
                        mm.then_inc(turned, 1)
                for i in range(4):
                    dense_piece(piece(IN + 8 + i), i, B_IN + 2, 0)
                    if i == 1:
                        turn_latent(0, QC, 4, 0, 2 * B_IN + 4).then_inc(turned, 1)
                pe.wait_ge(lat_ready, QC + KVC)
                with pe.Fori(0, 2) as n:
                    for e in range(2):
                        for i in range(4):
                            dense_piece(piece(IN + 12 + 4 * e + i, n, 8), i, n * 2 + (B_IN + 3 + e), 1 - e)
                            if i == 1:
                                turn_qk(2 * n + e)
                for i in range(4):
                    dense_piece(piece(IN + 28 + i), i, B_IN + 7, 1)

            def latent_block(pc, blk, first, chunks, rhs, width):
                pe.wait_ge(lo_ready, pc.index + 1)
                pe.wait_ge(taken, 2 * blk - 2)
                rhs_hi, rhs_lo = rhs
                for c in range(chunks):
                    for t in range(TILES):
                        mm = three_passes(result(blk, t)[:, 0:width], lat_hi[:, first + c, tile_of(t)],
                                          lat_lo[:, first + c, tile_of(t)], rhs_hi[:, c, :], rhs_lo[:, c, :],
                                          start=(c == 0), stop=(c == chunks - 1))
                return mm

            def turn_q2(j):
                pe.wait_ge(taken, 2 * (B_UQ + j) + 2)
                pe.wait_ge(kept, K_UQ + j)
                for t in range(TILES):
                    for h in range(2):
                        nc.tensor.transpose(banks[:, 4 + t, tile_of(h)], turn_in[:, t, tile_of(h)], ident[:, :])
                        at = 2 * HD + h * ROPE
                        mm = nc.tensor.transpose(banks[0:ROPE, 4 + t, tile_of(2 + h)],
                                                 turn_in[:, t, at:at + ROPE], ident[:, :])
                mm.then_inc(turned, 1)

            def turn_k2(j):
                pe.wait_ge(taken, 2 * (B_UKV + j) + 2)
                pe.wait_ge(kept, K_UKV + j)
                for t in range(TILES):
                    for h in range(2):
                        mm = nc.tensor.transpose(banks[:, 4 + t, tile_of(h)], turn_in[:, t, tile_of(h)], ident[:, :])
                mm.then_inc(turned, 1)

            def latent_up():
                width = 2 * (HD + ROPE)
                for j in range(UQ_BLOCKS):
                    pc = piece(UQ + j)
                    rhs = [cut(w, pc.split, QC, width) for w in (w_hi, w_lo)]
                    latent_block(pc, B_UQ + j, 0, QC, rhs, width).then_inc(piece_used, 1)
                    if j >= 1:
                        turn_q2(j - 1)
                for j in range(UKV_BLOCKS):
                    pc = piece(UKV + j // 2)
                    rhs = [cut(w, pc.split, KVC, 2 * BANK)[:, :, quarter(j % 2)] for w in (w_hi, w_lo)]
                    mm = latent_block(pc, B_UKV + j, QC, KVC, rhs, BANK)
                    mm.then_inc(piece_used if j % 2 else kv_half, 1)
                    if j == 0:
                        turn_q2(UQ_BLOCKS - 1)
                    else:
                        turn_k2(j - 1)
                turn_k2(UKV_BLOCKS - 1)

            def scores(u):
                s = banks[:, u % 2, :]
                if u >= 2:
                    pe.wait_ge(peaked, u - 1)
                h = u % HEADS
                for t, at in ((0, slice(0, P)), (1, slice(P, 3 * P))):
                    keys = slice(0, (t + 1) * P)
                    if u < HEADS:
                        mm = nc.tensor.matmul(s[:, at], qkT[:, h, tile_of(t)], qkT[:, HEADS + h, keys],
                                              start=True, stop=True)
                    else:
                        nc.tensor.matmul(s[:, at], q2T[:, h, tile_of(t)], k2T[:, h, keys], start=True, stop=False)
                        mm = nc.tensor.matmul(s[:, at], q2pT[:, h, tile_of(t)], k2pT[:, keys], start=False, stop=True)
                mm.then_inc(scores_ready, 1)

            def turn_probs(u):
                a = u % 2
                pe.wait_ge(probs_ready, u + 1)
                if u >= 2:
                    pe.wait_ge(probs_kept, u - 1)
                for n in range(3):
                    mm = nc.tensor.transpose(banks[:, 2 + a, tile_of(n)], probs[:, a, tile_of(n)], ident[:, :])
                mm.then_inc(probs_turned, 1)

            def weigh_values(u):
                a, h = u % 2, u % HEADS
                values = v1 if u < HEADS else v2
                cols = slice(h * HD, (h + 1) * HD)
                pe.wait_ge(probs_kept, u + 1)
                if u >= 2:
                    pe.wait_ge(head_out, u - 1)
                nc.tensor.matmul(banks[:, 4 + a, 0:P], probsT[:, a, 0:P], values[:, 0, cols], start=True, stop=True)
                nc.tensor.matmul(banks[:, 4 + a, P:2 * P], probsT[:, a, P:2 * P], values[:, 0, cols],
                                 start=True, stop=False)
                nc.tensor.matmul(banks[:, 4 + a, P:2 * P], probsT[:, a, 2 * P:], values[:, 1, cols],
                                 start=False, stop=True).then_inc(head_ready, 1)

            def attention():
                pe.wait_ge(kept, K_GU2)
                pe.wait_ge(taken, 2 * B_OUT)
                for u in range(2 * HEADS + 2):
                    if u < 2 * HEADS:
                        scores(u)
                    if 1 <= u <= 2 * HEADS:
                        turn_probs(u - 1)
                    if u >= 2:
                        weigh_values(u - 2)

            def out_piece(pc, i, n, n_turn=None):
                pe.wait_ge(lo_ready, pc.index + 1)
                rhs_hi, rhs_lo = cut(w_hi, pc.split, 4, BANK), cut(w_lo, pc.split, 4, BANK)

                def chunk(j, t):
                    c = 4 * i + j
                    return three_passes(result(n, t), act_hi[:, c, tile_of(t)], act_lo[:, c, tile_of(t)],
                                        rhs_hi[:, j, :], rhs_lo[:, j, :], start=(c == 0), stop=(c == DC - 1))
                if i < 3:
                    for j in range(4):
                        if n_turn is not None:
                            pe.wait_ge(act_ready, DC * n_turn + 4 * i + j + 1)
                        for t in range(TILES):
                            mm = chunk(j, t)
                    mm.then_inc(piece_used, 1)
                else:
                    if n_turn is not None:
                        pe.wait_ge(act_ready, DC * (n_turn + 1))
                    for t in range(TILES):
                        for j in range(4):
                            mm = chunk(j, t)
                        mm.then_inc(piece_used if t else tile0_done, 1)

            def mix_out():
                turn(2, 0)
                turn(2, 1)
                out_piece(piece(OUT), 0, 0, 2)
                turn(2, 2)
                turn(2, 3)
                for i in range(1, 4):
                    out_piece(piece(OUT + i), i, 0, 2)
                for n in range(1, OUT_BLOCKS):
                    for i in range(4):
                        if i == 0 and n >= 2:
                            pe.wait_ge(squared, 16 + 2 * (n - 1))
                            pe.wait_ge(y_scaled, 4 + 2 * (n - 1))
                        out_piece(piece(OUT + 4 * n + i), i, n)

            pe.wait_ge(consts_made, 1)
            pe.wait_ge(gains_landed, 16)
            nc.tensor.transpose(banks[:, 7, 256:256 + G_ROWS], gain_in[:, :], ident[0:G_ROWS, 0:G_ROWS])\
              .then_inc(gains_turned, 1)
            pe.wait_ge(gains_kept, 1)
            gate_up(GU1, 0)
            down(GU1, DOWN1)
            mix_in()
            latent_up()
            attention()
            mix_out()
            gate_up(GU2, 3)
            down(GU2, DOWN2)


def rope_tables():
    parts = []
    for dim in (HD, ROPE):
        inv = (np.float32(1.0) / (np.float32(10000.0) ** (np.arange(0, dim, 2, dtype=np.float32) / np.float32(dim))))
        ang = np.arange(TOKENS, dtype=np.float32)[:, None] * inv.astype(np.float32)[None, :]
        parts += [np.cos(ang), -np.sin(ang), np.sin(ang)]
    return np.concatenate(parts, axis=1).astype(np.float32)


def lay_out_weights(w):
    stream = np.zeros((P, PIECES, PIECE), np.float32)

    def put(first, a):
        groups, cols, chunks, _, width = a.shape
        a = a.transpose(3, 1, 0, 2, 4).reshape(P, cols * groups, chunks * width)
        stream[:, first:first + cols * groups, 0:chunks * width] = a

    def cut_up(m, chunks, width):
        rows, cols = m.shape
        return m.reshape(rows // (chunks * P), chunks, P, cols // width, width).transpose(0, 3, 1, 2, 4)

    for n, gu, dn in ((1, GU1, DOWN1), (2, GU2, DOWN2)):
        gate, up = (cut_up(w[f"ffn{n}_w_{k}"][0], 4, FB) for k in ("gate", "up"))
        put(gu, np.concatenate([gate, up], axis=4))
        put(dn, cut_up(w[f"ffn{n}_w_down"][0], 2, D // 2))
    w_in = w["w_in"][0]
    rest = Q_RANK + LAT
    put(IN, cut_up(w_in[:, Q_RANK:rest], 4, LAT))
    put(IN + 4, cut_up(w_in[:, 0:Q_RANK], 4, BANK))
    put(IN + 8, cut_up(w_in[:, rest:], 4, BANK))
    put(UQ, cut_up(w["mla_w_uq"][0], QC, UQ_WIDTH))
    put(UKV, cut_up(w["mla_w_ukv"][0], KVC, 2 * BANK))
    put(OUT, cut_up(w["w_out"][0], 4, BANK))
    return stream


def kernel(**inputs):
    import concourse.bacc as bacc
    from concourse.bass_utils import run_bass_kernel_spmd

    w = {name: np.asarray(a) for name, a in inputs.items()}
    x = np.ascontiguousarray(w["x"])
    gains = [w[n][0] for n in ("ffn1_pre_g", "mix_pre_g", "mla_out_g", "moba_out_g", "ffn2_pre_g",
                               "mla_q_norm_g", "mla_kv_norm_g")]
    arrays = {
        "x": x,
        "x_turned": np.ascontiguousarray(x[0].reshape(TOKENS, DC, P).transpose(2, 1, 0)),
        "weights": lay_out_weights(w),
        "gains": np.concatenate(gains).reshape(G_ROWS, P),
        "post_gains": np.concatenate([w["ffn1_post_g"], w["mix_post_g"], w["ffn2_post_g"]]),
        "rope": rope_tables(),
    }
    nc = bacc.Bacc("TRN2", target_bir_lowering=False, num_devices=1)
    args = [nc.dram_tensor(f"in_{n}", a.shape, F32, kind="ExternalInput").ap() for n, a in arrays.items()]
    args.append(nc.dram_tensor("out_rows", (1, TOKENS, D), F32, kind="ExternalOutput").ap())
    build_layer(nc, *args)
    ins = {f"in_{n}": a for n, a in arrays.items()}
    return run_bass_kernel_spmd(nc, [ins], core_ids=[0]).results[0]["out_rows"]
```

```python
from collections import namedtuple
from contextlib import ExitStack

import numpy as np

import concourse.bass as bass
from concourse import mybir

P = 128
TILES = 2
TOKENS = P * TILES
D = 2048
DC = D // P
FFN = 5632
FB = 256
N_FB = FFN // FB
FC = FFN // P
HEADS = 8
HD = 128
ROPE = 64
Q_RANK, KV_RANK = 512, 256
QC, KVC = Q_RANK // P, KV_RANK // P
BANK = 512
RAW = 4
PIECE = 2048
EPS = 1e-6
MASKED = -1e30
MOBA_SCALE = float(HD) ** -0.5
MLA_SCALE = float(HD + ROPE) ** -0.5

IN_BLOCKS, UQ_BLOCKS, UKV_BLOCKS, OUT_BLOCKS = 8, 4, 4, 4
LAT = KV_RANK + ROPE
UQ_WIDTH = 2 * (HD + ROPE)
GU1 = 0
DOWN1 = GU1 + 4 * N_FB
IN = DOWN1 + FC
UQ = IN + 4 * IN_BLOCKS
UKV = UQ + UQ_BLOCKS
OUT = UKV + UKV_BLOCKS
GU2 = OUT + 4 * OUT_BLOCKS
DOWN2 = GU2 + 4 * N_FB
PIECES = DOWN2 + FC
HALF = FC // 2

B_GU1 = 0
B_IN = B_GU1 + N_FB
B_UQ = B_IN + IN_BLOCKS
B_UKV = B_UQ + UQ_BLOCKS
B_OUT = B_UKV + UKV_BLOCKS
B_GU2 = B_OUT

T_GU1 = 0
T_CQ = T_GU1 + N_FB
T_CKV = T_CQ + 1
T_QK = T_CKV + 1
T_UQ = T_QK + 4
T_UKV = T_UQ + UQ_BLOCKS
T_GU2 = T_UKV + UKV_BLOCKS

K_GU1 = T_GU1
K_QK, K_UQ, K_UKV, K_GU2 = T_QK - 1, T_UQ - 1, T_UKV - 1, T_GU2 - 1

G_Q, G_KV = 4 * DC, 4 * DC + QC
G_ROWS = 4 * DC + QC + KVC

MOBA_TAB, MLA_TAB = 3 * HD // 2, 3 * ROPE // 2

(R_PRE1, R_POST1, R_PRE_MIX, R_Q, R_KV, R_MOBA, R_MLA, R_POST_MIX, R_PRE2, R_POST2) = range(10)

ALU = mybir.AluOpType
ACT = mybir.ActivationFunctionType
F32 = mybir.dt.float32
F32R = mybir.dt.float32r
BF16 = mybir.dt.bfloat16

Piece = namedtuple("Piece", "index slot fills split")


def piece(first, i=0, step=0):
    return Piece(first + step * i, first % RAW, first // RAW + (step // RAW) * i, first % 2)


def build_layer(nc, x, xT_in, stream, gains, post_gains, rope, out):
    ctx = ExitStack()
    with ctx:
        def sb(name, shape, dt=F32, stack=ctx):
            return stack.enter_context(nc.sbuf_tensor(name, shape, dt))

        def sem(name):
            return ctx.enter_context(nc.semaphore(name))

        rows = sb("rows", [P, TILES, D])
        raw = sb("raw", [P, RAW, PIECE])
        w_hi = sb("w_hi", [P, 2, PIECE], F32R)
        w_lo = sb("w_lo", [P, 2, PIECE], F32R)
        gain_row = sb("gain_row", [P, D])
        ident = sb("ident", [P, P])
        mask = sb("mask", [P, 2 * P])
        gain_in = sb("gain_in", [G_ROWS, P])
        gain = sb("gain", [P, G_ROWS])
        tab = sb("tab", [P, TILES, MOBA_TAB + MLA_TAB])
        probs = sb("probs", [P, 2, 3 * P])
        sumsq = sb("sumsq", [P, TILES, 4])
        var = sb("var", [P, 10, TILES])
        rs = sb("rs", [P, 10, TILES])
        minus_half = sb("minus_half", [P, TILES])
        peak = sb("peak", [P, 2, TILES])
        shift = sb("shift", [P, 2, TILES])
        total = sb("total", [P, 2, TILES])
        rtotal = sb("rtotal", [P, 2, TILES])

        with ExitStack() as s:
            act_hi = sb("act_hi", [P, DC, TOKENS], F32R, s)
            act_lo = sb("act_lo", [P, DC, TOKENS], F32R, s)
        q2T = sb("q2T", [P, HEADS, TOKENS])
        k2T = sb("k2T", [P, HEADS, TOKENS])
        q2pT = sb("q2pT", [ROPE, HEADS, TOKENS])
        v2 = sb("v2", [P, TILES, HEADS * HD])

        with ExitStack() as s:
            hidT = sb("hidT", [P, FC, TOKENS], F32, s)
        with ExitStack() as s:
            mix_hi = sb("mix_hi", [P, DC // 2, TOKENS], F32R, s)
            mix_lo = sb("mix_lo", [P, DC // 2, TOKENS], F32R, s)
        qkT = sb("qkT", [P, 2 * HEADS, TOKENS])
        v1 = sb("v1", [P, TILES, HEADS * HD])
        heads = sb("heads", [P, TILES, D])
        k2pT = sb("k2pT", [ROPE, TOKENS])
        tab_r = sb("tab_r", [P, TILES, MOBA_TAB])
        tab_q = sb("tab_q", [P, TILES, MLA_TAB])
        sb("hid_pad", [P, 192])

        with ExitStack() as s:
            hid_split = sb("hid_split", [P, 2, 2, 2, TOKENS], F32R, s)
            silu = sb("silu", [P, TILES, FB], F32, s)
            hid = sb("hid", [P, TILES, FB], F32, s)
        with ExitStack() as s:
            sb("junk_at", [P, 2, 2, 2, TOKENS], F32, s)
            junk = sb("junk", [P, D], BF16, s)
        lat_hi = sb("lat_hi", [P, QC + KVC, TOKENS], F32R)
        lat_lo = sb("lat_lo", [P, QC + KVC, TOKENS], F32R)

        with ExitStack() as s:
            xT = sb("xT", [P, DC, TOKENS], F32, s)
        with ExitStack() as s:
            scaled = sb("scaled", [P, TILES, D], F32, s)
        with ExitStack() as s:
            lat = sb("lat", [P, TILES, Q_RANK + KV_RANK + ROPE], F32, s)
        masked = sb("masked", [P, 2, 3 * P])
        probsT = sb("probsT", [P, 2, 3 * P])
        sb("lat_pad", [P, 128])
        turn_in = sb("turn_in", [P, TILES, BANK])
        rot_a = sb("rot_a", [P, BANK])
        rot_b = sb("rot_b", [P, BANK])
        sb("scaled_pad", [P, 384])
        junk_mix = probs[:, 0, 0:256].bitcast(BF16)

        banks = ctx.enter_context(nc.psum_tensor("banks", [P, 8, BANK], F32))

        xT_landed = [sem(f"xT_landed{k}") for k in range(4)]
        rows_landed = [sem(f"rows_landed{t}") for t in range(TILES)]
        gains_landed = sem("gains_landed")
        tab_landed = sem("tab_landed")
        gain_row_landed = sem("gain_row_landed")
        raw_landed = [sem(f"raw_landed{s}") for s in range(RAW)]
        stored = sem("stored")
        zeroed = sem("zeroed")
        consts_made = sem("consts_made")
        gains_turned = sem("gains_turned")
        gains_kept = sem("gains_kept")
        hi_ready = sem("hi_ready")
        lo_ready = sem("lo_ready")
        hid_hi_ready = sem("hid_hi_ready")
        piece_used = sem("piece_used")
        tile0_done = sem("tile0_done")
        rows_ready = sem("rows_ready")
        quad_turned = sem("quad_turned")
        act_hi_ready = sem("act_hi_ready")
        act_ready = sem("act_ready")
        squared = sem("squared")
        var_ready = sem("var_ready")
        rs_ready = sem("rs_ready")
        silu_ready = sem("silu_ready")
        taken = sem("taken")
        turned = sem("turned")
        kept = sem("kept")
        tab_scaled = sem("tab_scaled")
        rot_step = sem("rot_step")
        pe_rows = sem("pe_rows")
        lat_hi_ready = sem("lat_hi_ready")
        lat_ready = sem("lat_ready")
        first_landed = sem("first_landed")
        first_hi_ready = sem("first_hi_ready")
        first_lo_ready = sem("first_lo_ready")
        y_scaled = sem("y_scaled")
        scores_ready = sem("scores_ready")
        peaked = sem("peaked")
        shifted = sem("shifted")
        probs_ready = sem("probs_ready")
        probs_turned = sem("probs_turned")
        probs_kept = sem("probs_kept")
        head_ready = sem("head_ready")
        totalled = sem("totalled")
        head_out = sem("head_out")

        x_dram = x.rearrange("b (t p) d -> p (b t) d", p=P)
        out_dram = out.rearrange("b (t p) d -> p (b t) d", p=P)

        def cut(t, slot, chunks, width):
            return t[:, slot, 0:chunks * width].rearrange("p (c n) -> p c n", c=chunks)

        def result(block, t):
            return banks[:, 2 * (block % 2) + t, :]

        def tile_of(t):
            return slice(t * P, (t + 1) * P)

        def quarter(k):
            return slice(k * BANK, (k + 1) * BANK)

        def down_banks(half, t):
            return ((6, 0), (2, 4))[half][t]

        def turn_at(turn, k, j):
            bank = ((0, 6, 4, 6) if turn == 2 else (6, 4, 6, 4))[k] + j // 2
            return banks[:, bank, (j % 2) * TOKENS:(j % 2 + 1) * TOKENS]

        def act_split(turn, c):
            if turn == 2 and c < DC // 2:
                return mix_hi[:, c, :], mix_lo[:, c, :]
            return act_hi[:, c, :], act_lo[:, c, :]

        def turned_chunk(turn, c):
            return xT[:, c, :] if turn == 0 else turn_at(turn, c // 4, c % 4)

        def rs_of(job, t=TILES - 1):
            return TILES * job + t + 1

        block = ctx.enter_context(nc.Block())

        @block.sync
        def _(sp):
            def raw_free(pc):
                if not (isinstance(pc.index, int) and pc.index < RAW):
                    sp.wait_ge(lo_ready, pc.index - RAW + 1)

            def load(pc, width=PIECE):
                raw_free(pc)
                sp.dma_start(raw[:, pc.slot, 0:width], stream[bass.ds(pc.index, 1), :, 0:width]
                             .rearrange("o p n -> (o p) n")).then_inc(raw_landed[pc.slot], 16)

            def load_from(first, end):
                with sp.Fori(0, (end - first) // RAW) as i:
                    for n in range(RAW):
                        load(piece(first + n, i, RAW))

            def load_gain_row(n, uses):
                sp.wait_ge(y_scaled, uses)
                sp.dma_start(gain_row[:, :], post_gains[n, :].partition_broadcast(P)).then_inc(gain_row_landed, 16)

            sp.dma_start(raw[:, 0, 0:PIECE // 2], stream[0, :, 0:PIECE // 2]).then_inc(first_landed, 16)
            for n in range(RAW):
                if n:
                    load(piece(n))
                sp.dma_start(xT[:, 4 * n:4 * n + 4, :], xT_in[:, 4 * n:4 * n + 4, :]).then_inc(xT_landed[n], 16)
                if n == 0:
                    sp.dma_start(raw[:, 0, PIECE // 2:], stream[0, :, PIECE // 2:]).then_inc(raw_landed[0], 16)
            for n in range(RAW, 2 * RAW):
                load(piece(n))
                if n - RAW < TILES:
                    sp.dma_start(rows[:, n - RAW, :], x_dram[:, n - RAW, :]).then_inc(rows_landed[n - RAW], 16)
            sp.dma_start(gain_row[:, :], post_gains[0, :].partition_broadcast(P)).then_inc(gain_row_landed, 16)
            sp.dma_start(tab[:, :, :], rope.rearrange("(t p) n -> p t n", p=P)).then_inc(tab_landed, 16)
            load_from(2 * RAW, IN + 4)
            for n in range(4, 8):
                load(piece(IN + n), 4 * LAT)
            load_from(IN + 8, IN + 12)
            load_gain_row(1, 4)
            load_from(IN + 12, UQ)
            for n in range(UQ_BLOCKS):
                load(piece(UQ + n), QC * UQ_WIDTH)
            for n in range(UKV_BLOCKS):
                load(piece(UKV + n), KVC * BANK)
            load_from(OUT, GU2 + 4)
            load_gain_row(2, 4 + 2 * OUT_BLOCKS)
            load_from(GU2 + 4, PIECES)
            for t in range(TILES):
                for k in range(4):
                    sp.wait_ge(rows_ready, 24 + 4 * t + k + 1)
                    sp.dma_start(out_dram[:, t, quarter(k)], rows[:, t, quarter(k)]).then_inc(stored, 16)
            sp.wait_ge(stored, 16 * 4 * TILES)

        @block.gpsimd
        def _(pool):
            nc.gpsimd.memset(ident[:, :], 0.0)
            nc.gpsimd.memset(mask[:, :], 0.0)
            nc.gpsimd.memset(minus_half[:, :], -0.5).then_inc(zeroed, 1)
            pool.wait_ge(zeroed, 1)
            nc.gpsimd.affine_select(out=ident[:, :], in_=ident[:, :], compare_op=ALU.not_equal, fill=1.0,
                                    base=0, pattern=[[-1, P]], channel_multiplier=1)
            nc.gpsimd.affine_select(out=mask[:, P:2 * P], in_=mask[:, P:2 * P], compare_op=ALU.is_ge,
                                    fill=MASKED, base=0, pattern=[[-1, P]], channel_multiplier=1)\
              .then_inc(consts_made, 1)

            steps, sums = [0], [0]

            def step(ins):
                ins.then_inc(var_ready, 1)
                steps[0] += 1
                pool.wait_ge(var_ready, steps[0])

            def inverse_rms(job, parts, width, factor, col=0):
                c = factor ** -2
                for n in range(parts):
                    for t in range(TILES):
                        sums[0] += 1
                        pool.wait_ge(squared, sums[0])
                        one = slice(t, t + 1)
                        if n == 0:
                            step(nc.gpsimd.tensor_scalar(var[:, job, one], sumsq[:, one, col], c / width, c * EPS,
                                                         ALU.mult, ALU.add))
                        else:
                            step(nc.gpsimd.tensor_scalar(var[:, job, one], sumsq[:, one, n], c / width,
                                                         var[:, job, one], ALU.mult, ALU.add))
                        if n == parts - 1:
                            nc.gpsimd.tensor_tensor(rs[:, job, one], var[:, job, one], minus_half[:, one], ALU.pow)\
                              .then_inc(rs_ready, 1)

            inverse_rms(R_PRE1, 1, D, 1.0)
            inverse_rms(R_POST1, 2, D, 0.5)
            inverse_rms(R_PRE_MIX, 1, D, 1.0)
            inverse_rms(R_Q, 1, Q_RANK, 1.0, col=3)
            inverse_rms(R_KV, 1, KV_RANK, 1.0, col=2)
            inverse_rms(R_MOBA, 1, HEADS * HD, 1.0, col=0)
            inverse_rms(R_MLA, 1, HEADS * HD, 1.0, col=1)
            inverse_rms(R_POST_MIX, OUT_BLOCKS, D, 1.0)
            inverse_rms(R_PRE2, 1, D, 1.0)
            inverse_rms(R_POST2, 2, D, 0.5)

        @block.scalar
        def _(act):
            def take_high(pc, width=PIECE):
                act.wait_ge(raw_landed[pc.slot], 16 * (pc.fills + 1))
                if not (isinstance(pc.index, int) and pc.index < 2):
                    act.wait_ge(piece_used, pc.index - 1)
                nc.scalar.activation(w_hi[:, pc.split, 0:width], raw[:, pc.slot, 0:width], ACT.Copy)\
                  .then_inc(hi_ready, 1)

            def turn_high(turn, k, chunks=range(4)):
                if turn == 0:
                    act.wait_ge(xT_landed[k], 16)
                else:
                    act.wait_ge(quad_turned, 4 * (turn - 1) + k + 1)
                for j in chunks:
                    c = 4 * k + j
                    nc.scalar.activation(act_split(turn, c)[0], turned_chunk(turn, c), ACT.Copy,
                                         scale=gain[:, DC * turn + c:DC * turn + c + 1]).then_inc(act_hi_ready, 1)

            squares = [0]

            def square(of, scratch, tile, col):
                if squares[0]:
                    act.wait_ge(squared, squares[0])
                nc.scalar.activation(scratch, of, ACT.Square, accum_out=sumsq[:, tile, col:col + 1])\
                  .then_inc(squared, 1)
                squares[0] += 1

            def gate(stage, b, parity):
                first, job = (B_GU1, R_PRE1) if stage == GU1 else (B_GU2, R_PRE2)
                if not (isinstance(b, int) and b == 0):
                    act.wait_ge(taken, 2 * first + 2 * b)
                for t in range(TILES):
                    nc.scalar.activation(silu[:, t, :], result(parity, t)[:, 0:FB], ACT.Silu,
                                         scale=rs[:, job, t:t + 1]).then_inc(silu_ready, 1)

            def keep_hidden(stage, b):
                first = T_GU1 if stage == GU1 else T_GU2
                act.wait_ge(turned, first + b + 1)
                nc.scalar.copy(hidT[:, bass.ds(2 * b, 2), :],
                               banks[:, 4, :].rearrange("p (c n) -> p c n", c=2)).then_inc(kept, 1)

            def gate_up(stage, turn):
                turn_high(turn, 0)
                if turn == 0:
                    act.wait_ge(raw_landed[0], 16)
                    nc.scalar.activation(w_hi[:, 0, PIECE // 2:], raw[:, 0, PIECE // 2:], ACT.Copy)\
                      .then_inc(hi_ready, 1)
                    take_high(piece(stage + 1))
                turn_high(turn, 1)
                take_high(piece(stage + 2))
                turn_high(turn, 2)
                if turn:
                    take_high(piece(stage + 3))
                turn_high(turn, 3)
                if turn == 0:
                    for t in range(TILES):
                        take_high(piece(stage + 3 + t))
                        act.wait_ge(rows_landed[t], 16)
                        square(rows[:, t, :], junk[:, :], t, 0)
                    take_high(piece(stage + 5))
                else:
                    for t in range(TILES):
                        square(rows[:, t, :], junk[:, :], t, 0)
                    take_high(piece(stage + 4))
                    take_high(piece(stage + 5))
                act.wait_ge(rs_ready, rs_of(R_PRE1 if stage == GU1 else R_PRE2))
                gate(stage, 0, 0)
                take_high(piece(stage + 6))
                take_high(piece(stage + 7))
                keep_hidden(stage, 0)
                with act.Fori(0, (N_FB - 2) // 2) as n:
                    for e in range(2):
                        for i in range(4):
                            take_high(piece(stage + 8 + 4 * e + i, n, 8))
                            if i == 1:
                                gate(stage, 2 * n + (e + 1), (e + 1) % 2)
                        keep_hidden(stage, 2 * n + (e + 1))

            def take_high_down(pc, n):
                act.wait_ge(raw_landed[pc.slot], 16 * (pc.fills + 1))
                act.wait_ge(piece_used, pc.index - 1)
                nc.scalar.activation(w_hi[:, pc.split, :], raw[:, pc.slot, :], ACT.Copy).then_inc(hi_ready, 1)
                nc.scalar.copy(hid_split[:, pc.split, 0], hidT[:, bass.ds(2 * n, 2), :]).then_inc(hid_hi_ready, 1)

            def square_down(stage, half):
                done = (half + 1) * HALF
                for t in range(TILES):
                    if t == 0:
                        act.wait_ge(tile0_done, done + (FC + OUT_BLOCKS if stage == DOWN2 else 0))
                    else:
                        act.wait_ge(piece_used, stage + done)
                    b = down_banks(half, t)
                    square(banks[:, b:b + 2, :].rearrange("p b n -> p (b n)"), junk[:, 0:D // 2], t, half)

            def down(gu_stage, stage):
                take_high_down(piece(stage), 0)
                take_high_down(piece(stage + 1), 1)
                gate(gu_stage, N_FB - 1, 1)
                keep_hidden(gu_stage, N_FB - 1)
                with act.Fori(0, (HALF - 2) // 4) as i:
                    for n in range(2, 6):
                        take_high_down(piece(stage + n, i, 4), 4 * i + n)
                take_high_down(piece(stage + HALF), 0)
                take_high_down(piece(stage + HALF + 1), 1)
                square_down(stage, 0)
                with act.Fori(0, (HALF - 2) // 4) as i:
                    for n in range(2, 6):
                        take_high_down(piece(stage + HALF + n, i, 4), 4 * i + n)

            def keep_qk(j):
                act.wait_ge(turned, T_QK + 1 + j)
                for t in range(TILES):
                    ins = nc.scalar.copy(qkT[:, bass.ds(4 * j, 4), tile_of(t)],
                                         banks[:, 4 + t, :].rearrange("p (h n) -> p h n", h=4))
                ins.then_inc(kept, 1)

            def latent_high(first, chunks, bank, g):
                for c in range(chunks):
                    nc.scalar.activation(lat_hi[:, first + c, :],
                                         banks[:, bank + c // 2, (c % 2) * TOKENS:(c % 2 + 1) * TOKENS],
                                         ACT.Copy, scale=gain[:, g + c:g + c + 1]).then_inc(lat_hi_ready, 1)

            def square_latent(tiles_taken, cols, col):
                act.wait_ge(taken, tiles_taken)
                for t in range(TILES):
                    square(lat[:, t, cols], junk_mix[:, 0:cols.stop - cols.start], t, col)

            def keep_q2(j):
                act.wait_ge(turned, T_UQ + j + 1)
                for t in range(TILES):
                    b = banks[:, 4 + t, :].rearrange("p (h n) -> p h n", h=4)
                    nc.scalar.copy(q2T[:, 2 * j:2 * j + 2, tile_of(t)], b[:, 0:2, :])
                    ins = nc.scalar.copy(q2pT[:, 2 * j:2 * j + 2, tile_of(t)], b[0:ROPE, 2:4, :])
                ins.then_inc(kept, 1)

            def keep_k2(j):
                act.wait_ge(turned, T_UKV + j + 1)
                for t in range(TILES):
                    b = banks[:, 4 + t, :].rearrange("p (h n) -> p h n", h=4)
                    ins = nc.scalar.copy(k2T[:, 2 * j:2 * j + 2, tile_of(t)], b[:, 0:2, :])
                ins.then_inc(kept, 1)

            def mix_in():
                turn_high(1, 0)
                turn_high(1, 1)
                take_high(piece(IN + 2))
                turn_high(1, 2)
                take_high(piece(IN + 3))
                turn_high(1, 3)
                for t in range(TILES):
                    square(rows[:, t, :], junk[:, :], t, 0)
                take_high(piece(IN + 4), 4 * LAT)
                take_high(piece(IN + 5), 4 * LAT)
                take_high(piece(IN + 6), 4 * LAT)
                take_high(piece(IN + 7), 4 * LAT)
                act.wait_ge(turned, T_CQ + 1)
                latent_high(0, QC, 4, G_Q)
                take_high(piece(IN + 8))
                take_high(piece(IN + 9))
                square_latent(2 * B_IN + 2, slice(0, Q_RANK), 3)
                square_latent(2 * B_IN + 4, slice(Q_RANK, Q_RANK + KV_RANK), 2)
                take_high(piece(IN + 10))
                take_high(piece(IN + 11))
                act.wait_ge(turned, T_CKV + 1)
                latent_high(QC, KVC, 6, G_KV)
                nc.scalar.copy(k2pT[:, :], banks[0:ROPE, 7, 0:TOKENS]).then_inc(kept, 1)
                with act.Fori(0, 2) as n:
                    for e in range(2):
                        for i in range(4):
                            take_high(piece(IN + 12 + 4 * e + i, n, 8))
                        keep_qk(2 * n + e)
                for i in range(4):
                    take_high(piece(IN + 28 + i))

            def take_high_half(pc, half):
                cols = slice(half * PIECE // 2, (half + 1) * PIECE // 2)
                if half == 0:
                    act.wait_ge(raw_landed[pc.slot], 16 * (pc.fills + 1))
                    act.wait_ge(piece_used, pc.index - 1)
                ins = nc.scalar.activation(w_hi[:, pc.split, cols], raw[:, pc.slot, cols], ACT.Copy)
                if half == 1:
                    ins.then_inc(hi_ready, 1)

            def latent_up():
                uq_width = QC * 2 * (HD + ROPE)
                for j in range(UQ_BLOCKS):
                    take_high(piece(UQ + j), uq_width)
                keep_q2(0)
                take_high(piece(UKV), KVC * BANK)
                keep_q2(1)
                take_high(piece(UKV + 1), KVC * BANK)
                keep_q2(2)
                take_high(piece(UKV + 2), KVC * BANK)
                keep_q2(3)
                take_high(piece(UKV + 3), KVC * BANK)
                keep_k2(0)
                keep_k2(1)
                exponentials(0)
                keep_k2(2)
                keep_k2(3)
                keep_probs(0)
                exponentials(1)

            def exponentials(u):
                a = u % 2
                scale = MOBA_SCALE if u < HEADS else MLA_SCALE
                act.wait_ge(shifted, u + 1)
                if u >= 2:
                    act.wait_ge(probs_turned, u - 1)
                    act.wait_ge(totalled, u - 1)
                nc.scalar.activation(probs[:, a, 0:P], masked[:, a, 0:P], ACT.Exp, bias=shift[:, a, 0:1],
                                     scale=scale, accum_out=total[:, a, 0:1])
                nc.scalar.activation(probs[:, a, P:], masked[:, a, P:], ACT.Exp, bias=shift[:, a, 1:2],
                                     scale=scale, accum_out=total[:, a, 1:2]).then_inc(probs_ready, 1)

            def keep_probs(u):
                a = u % 2
                act.wait_ge(probs_turned, u + 1)
                if u >= 2:
                    act.wait_ge(head_ready, u - 1)
                nc.scalar.copy(probsT[:, a, :], banks[:, 2 + a, 0:3 * P]).then_inc(probs_kept, 1)

            def square_heads(half, t):
                act.wait_ge(head_out, (half + 1) * HEADS)
                square(heads[:, t, half * D // 2:(half + 1) * D // 2], rot_a[:, :].bitcast(BF16), t, half)

            def attention():
                for u in range(2, 2 * HEADS + 2):
                    if u >= 3:
                        keep_probs(u - 2)
                    if u < 2 * HEADS:
                        exponentials(u)
                    if u in (HEADS, HEADS + 1):
                        take_high_half(piece(OUT), u - HEADS)
                    if u in (HEADS + 4, HEADS + 5):
                        take_high_half(piece(OUT + 1), u - HEADS - 4)
                    if u in (HEADS + 2, HEADS + 3):
                        square_heads(0, u - HEADS - 2)
                    if u in (HEADS + 6, HEADS + 7):
                        turn_high(2, 0, ((0, 1), (2, 3))[u - HEADS - 6])
                    if u == HEADS + 9:
                        turn_high(2, 1)
                for t in range(TILES):
                    square_heads(1, t)

            def square_out(n):
                for t in range(TILES):
                    if t == 0:
                        act.wait_ge(tile0_done, FC + n + 1)
                    else:
                        act.wait_ge(piece_used, OUT + 4 * n + 4)
                    square(result(n, t), junk[:, 0:BANK], t, n)

            def mix_out():
                take_high(piece(OUT + 2))
                turn_high(2, 2)
                take_high(piece(OUT + 3))
                turn_high(2, 3)
                for n in range(1, OUT_BLOCKS):
                    take_high(piece(OUT + 4 * n))
                    take_high(piece(OUT + 4 * n + 1))
                    square_out(n - 1)
                    take_high(piece(OUT + 4 * n + 2))
                    take_high(piece(OUT + 4 * n + 3))
                take_high(piece(GU2))
                square_out(OUT_BLOCKS - 1)
                take_high(piece(GU2 + 1))

            act.dma_start(gain_in[:, :], gains).then_inc(gains_landed, 16)
            act.wait_ge(first_landed, 16)
            nc.scalar.activation(w_hi[:, 0, 0:PIECE // 2], raw[:, 0, 0:PIECE // 2], ACT.Copy)\
              .then_inc(first_hi_ready, 1)
            act.wait_ge(gains_turned, 1)
            nc.scalar.copy(gain[:, :], banks[:, 7, 256:256 + G_ROWS]).then_inc(gains_kept, 1)
            act.wait_ge(gains_kept, 1)

            gate_up(GU1, 0)
            down(GU1, DOWN1)
            take_high(piece(IN))
            square_down(DOWN1, 1)
            take_high(piece(IN + 1))
            mix_in()
            latent_up()
            attention()
            mix_out()
            gate_up(GU2, 3)
            down(GU2, DOWN2)
            square_down(DOWN2, 1)

        @block.vector
        def _(dve):
            def take_low(pc, width=PIECE):
                dve.wait_ge(hi_ready, pc.index + 1)
                nc.vector.tensor_tensor(w_lo[:, pc.split, 0:width], raw[:, pc.slot, 0:width],
                                        w_hi[:, pc.split, 0:width], ALU.subtract).then_inc(lo_ready, 1)

            def turn_low(turn, k, chunks=range(4)):
                for j in chunks:
                    c = 4 * k + j
                    if j % 2 == 0:
                        dve.wait_ge(act_hi_ready, DC * turn + c + 2)
                    nc.vector.scalar_tensor_tensor(
                        out=act_split(turn, c)[1], in0=turned_chunk(turn, c),
                        scalar=gain[:, DC * turn + c:DC * turn + c + 1], in1=act_split(turn, c)[0], op0=ALU.mult, op1=ALU.subtract).then_inc(act_ready, 1)

            def multiply_hidden(stage, b, parity):
                turns, job, before = (T_GU1, R_PRE1, 0) if stage == GU1 else (T_GU2, R_PRE2, N_FB)
                if not (isinstance(b, int) and b == 0):
                    dve.wait_ge(turned, turns + b)
                for t in range(TILES):
                    dve.wait_ge(silu_ready, b * 2 + (2 * before + t + 1))
                    nc.vector.scalar_tensor_tensor(
                        out=hid[:, t, :], in0=result(parity, t)[:, FB:], scalar=rs[:, job, t:t + 1],
                        in1=silu[:, t, :], op0=ALU.mult, op1=ALU.mult).then_inc(taken, 1)

            def add_residual(job, turn, scale_last, following=None):
                def add(k, t):
                    if k == 0:
                        scale_last(t)
                        dve.wait_ge(rs_ready, rs_of(job, t))
                        dve.wait_ge(y_scaled, scaled_parts[job] - 1 + t)
                    nc.vector.scalar_tensor_tensor(
                        out=rows[:, t, quarter(k)], in0=scaled[:, t, quarter(k)], scalar=rs[:, job, t:t + 1],
                        in1=rows[:, t, quarter(k)], op0=ALU.mult, op1=ALU.add).then_inc(rows_ready, 1)

                if turn is None:
                    for t in range(TILES):
                        for k in range(4):
                            add(k, t)
                    return
                for k in range(4):
                    for t in range(TILES):
                        add(k, t)
                    if k >= 1:
                        if k == 3:
                            take_low(piece(following + 2))
                        turn_low(turn, k - 1)
                    if k == 1:
                        take_low(piece(following + 1))
                take_low(piece(following + 3))
                turn_low(turn, 3)

            scaled_parts = {R_POST1: 4, R_POST_MIX: 4 + 2 * OUT_BLOCKS, R_POST2: 8 + 2 * OUT_BLOCKS}

            def gate_up(stage):
                take_low(piece(stage + 4))
                take_low(piece(stage + 5))
                dve.wait_ge(rs_ready, rs_of(R_PRE1 if stage == GU1 else R_PRE2))
                multiply_hidden(stage, 0, 0)
                take_low(piece(stage + 6))
                take_low(piece(stage + 7))
                with dve.Fori(0, (N_FB - 2) // 2) as n:
                    for e in range(2):
                        for i in range(4):
                            take_low(piece(stage + 8 + 4 * e + i, n, 8))
                            if i == 1:
                                multiply_hidden(stage, 2 * n + (e + 1), (e + 1) % 2)

            def take_low_down(pc, n, hid_base):
                dve.wait_ge(hi_ready, pc.index + 1)
                nc.vector.tensor_tensor(w_lo[:, pc.split, :], raw[:, pc.slot, :], w_hi[:, pc.split, :],
                                        ALU.subtract)
                dve.wait_ge(hid_hi_ready, pc.index - hid_base + 1)
                nc.vector.tensor_tensor(hid_split[:, pc.split, 1], hidT[:, bass.ds(2 * n, 2), :],
                                        hid_split[:, pc.split, 0], ALU.subtract).then_inc(lo_ready, 1)

            def scale_down(half, sums_before, t):
                cols = slice(half * D // 2, (half + 1) * D // 2)
                dve.wait_ge(squared, sums_before + t + 1)
                b = down_banks(half, t)
                nc.vector.tensor_tensor(scaled[:, t, cols], banks[:, b:b + 2, :].rearrange("p b n -> p (b n)"),
                                        gain_row[:, cols], ALU.mult).then_inc(y_scaled, 1)

            def down(gu_stage, stage, sums_before, gain_loads):
                base = DOWN1 if stage == DOWN1 else DOWN2 - FC
                take_low_down(piece(stage), 0, base)
                take_low_down(piece(stage + 1), 1, base)
                multiply_hidden(gu_stage, N_FB - 1, 1)
                with dve.Fori(0, (HALF - 2) // 4) as i:
                    for n in range(2, 6):
                        take_low_down(piece(stage + n, i, 4), 4 * i + n, base)
                take_low_down(piece(stage + HALF), 0, base)
                take_low_down(piece(stage + HALF + 1), 1, base)
                dve.wait_ge(gain_row_landed, 16 * gain_loads)
                for t in range(TILES):
                    scale_down(0, sums_before, t)
                with dve.Fori(0, (HALF - 2) // 4) as i:
                    for n in range(2, 6):
                        take_low_down(piece(stage + HALF + n, i, 4), 4 * i + n, base)

            def rotate(to, of, table, n_heads, half):
                def by_head(ap):
                    return ap.rearrange("p (h a d) -> p h a d", h=n_heads, a=2)
                n = n_heads * 2 * half
                a, b = by_head(rot_a[:, 0:n]), by_head(rot_b[:, 0:n])

                def bc(lo, reps):
                    shape = [P, n_heads] + reps + [half]
                    t = table[:, lo:lo + half].unsqueeze(1)
                    if reps:
                        t = t.unsqueeze(1)
                    return t.to_broadcast(shape)
                nc.vector.tensor_tensor(a, of, bc(0, [2]), ALU.mult)
                nc.vector.tensor_tensor(b[:, :, 0, :], of[:, :, 1, :], bc(half, []), ALU.mult)
                nc.vector.tensor_tensor(b[:, :, 1, :], of[:, :, 0, :], bc(2 * half, []), ALU.mult)\
                  .then_inc(rot_step, 1)
                return a, b, to

            def rotate_done(a, b, to, count):
                dve.wait_ge(rot_step, count)
                return nc.vector.tensor_tensor(to, a, b, ALU.add)

            def rotate_qk(j, parity):
                dve.wait_ge(piece_used, j * 4 + (IN + 4 * 3))
                dve.wait_ge(turned, T_QK + j)
                for t in range(TILES):
                    if t == 1:
                        dve.wait_ge(taken, j * 2 + (2 * (B_IN + 2) + 1))
                    of = result(parity, t).rearrange("p (h a d) -> p h a d", h=4, a=2)
                    to = turn_in[:, t, :].rearrange("p (h a d) -> p h a d", h=4, a=2)
                    a, b, to = rotate(to, of, tab_r[:, t, :], 4, HD // 2)
                    rotate_done(a, b, to, j * 2 + (2 + t + 1)).then_inc(taken, 1)

            def scale_latent(b, width, at):
                dve.wait_ge(piece_used, IN + 4 * (b + 1))
                for t in range(TILES):
                    nc.vector.tensor_scalar(lat[:, t, at:at + width], result(b, t)[:, 0:width],
                                            rs[:, R_PRE_MIX, t:t + 1], None, ALU.mult).then_inc(taken, 1)

            def latent_low(first, chunks, bank, g):
                for c in range(chunks):
                    if c % 2 == 0:
                        dve.wait_ge(lat_hi_ready, first + c + 2)
                    nc.vector.scalar_tensor_tensor(
                        out=lat_lo[:, first + c, :],
                        in0=banks[:, bank + c // 2, (c % 2) * TOKENS:(c % 2 + 1) * TOKENS],
                        scalar=gain[:, g + c:g + c + 1], in1=lat_hi[:, first + c, :],
                        op0=ALU.mult, op1=ALU.subtract).then_inc(lat_ready, 1)

            def scale_v1(n, parity):
                dve.wait_ge(piece_used, IN + 4 * (7 + n))
                for t in range(TILES):
                    nc.vector.tensor_scalar(v1[:, t, quarter(n)], result(parity, t),
                                            rs[:, R_PRE_MIX, t:t + 1], None, ALU.mult).then_inc(taken, 1)

            def mix_in():
                take_low(piece(IN + 4), 4 * LAT)
                take_low(piece(IN + 5), 4 * LAT)
                dve.wait_ge(rs_ready, rs_of(R_PRE_MIX))
                scale_latent(0, Q_RANK, 0)
                take_low(piece(IN + 6), 4 * LAT)
                take_low(piece(IN + 7), 4 * LAT)
                latent_low(0, QC, 4, G_Q)
                take_low(piece(IN + 8))
                take_low(piece(IN + 9))
                scale_latent(1, LAT, Q_RANK)
                dve.wait_ge(tab_landed, 16)
                dve.wait_ge(taken, 2 * B_IN + 4)
                for t in range(TILES):
                    at = Q_RANK + KV_RANK
                    if t == 1:
                        dve.wait_ge(pe_rows, 1)
                    of = lat[:, t, at:at + ROPE].rearrange("p (h a d) -> p h a d", h=1, a=2)
                    to = turn_in[:, t, 0:ROPE].rearrange("p (h a d) -> p h a d", h=1, a=2)
                    a, b, to = rotate(to, of, tab[:, t, MOBA_TAB:], 1, ROPE // 2)
                    rotate_done(a, b, to, t + 1).then_inc(pe_rows, 1)
                take_low(piece(IN + 10))
                take_low(piece(IN + 11))
                for t in range(TILES):
                    nc.vector.tensor_scalar(tab_r[:, t, :], tab[:, t, 0:MOBA_TAB], rs[:, R_PRE_MIX, t:t + 1],
                                            None, ALU.mult).then_inc(tab_scaled, 1)
                latent_low(QC, KVC, 6, G_KV)
                dve.wait_ge(tab_scaled, 2)
                with dve.Fori(0, 2) as n:
                    for e in range(2):
                        for i in range(4):
                            take_low(piece(IN + 12 + 4 * e + i, n, 8))
                            if i == 1:
                                rotate_qk(2 * n + e, e)
                take_low(piece(IN + 28))
                take_low(piece(IN + 29))
                scale_v1(0, 0)
                take_low(piece(IN + 30))
                take_low(piece(IN + 31))

            def split_q2(j):
                dve.wait_ge(piece_used, UQ + j + 1)
                dve.wait_ge(turned, T_UQ + j)
                for t in range(TILES):
                    if t == 1:
                        dve.wait_ge(taken, 2 * (B_UQ + j) + 1)
                    of = result(j, t)[:, 0:2 * (HD + ROPE)].rearrange("p (h n) -> p h n", h=2)
                    nc.vector.tensor_scalar(turn_in[:, t, 0:2 * HD].rearrange("p (h n) -> p h n", h=2),
                                            of[:, :, 0:HD], rs[:, R_Q, t:t + 1], None, ALU.mult)
                    to = turn_in[:, t, 2 * HD:2 * HD + 2 * ROPE].rearrange("p (h a d) -> p h a d", h=2, a=2)
                    a, b, to = rotate(to, of[:, :, HD:].rearrange("p h (a d) -> p h a d", a=2),
                                      tab_q[:, t, :], 2, ROPE // 2)
                    rotate_done(a, b, to, 10 + 2 * j + t + 1).then_inc(taken, 1)

            def split_kv2(j):
                dve.wait_ge(turned, T_UKV + j)
                dve.wait_ge(piece_used, UKV + j + 1)
                for t in range(TILES):
                    of = result(j, t).rearrange("p (h n) -> p h n", h=2)
                    nc.vector.tensor_scalar(turn_in[:, t, 0:2 * HD].rearrange("p (h n) -> p h n", h=2),
                                            of[:, :, 0:HD], rs[:, R_KV, t:t + 1], None, ALU.mult)
                    nc.vector.tensor_scalar(v2[:, t, 2 * j * HD:(2 * j + 2) * HD].rearrange("p (h n) -> p h n", h=2),
                                            of[:, :, HD:], rs[:, R_KV, t:t + 1], None, ALU.mult).then_inc(taken, 1)

            def latent_up():
                uq_width = QC * 2 * (HD + ROPE)
                dve.wait_ge(rs_ready, rs_of(R_KV))
                for t in range(TILES):
                    nc.vector.tensor_scalar(tab_q[:, t, :], tab[:, t, MOBA_TAB:], rs[:, R_Q, t:t + 1],
                                            None, ALU.mult).then_inc(tab_scaled, 1)
                take_low(piece(UQ), uq_width)
                take_low(piece(UQ + 1), uq_width)
                scale_v1(1, 1)
                dve.wait_ge(tab_scaled, 4)
                split_q2(0)
                take_low(piece(UQ + 2), uq_width)
                split_q2(1)
                take_low(piece(UQ + 3), uq_width)
                split_q2(2)
                take_low(piece(UKV), KVC * BANK)
                split_q2(3)
                take_low(piece(UKV + 1), KVC * BANK)
                split_kv2(0)
                take_low(piece(UKV + 2), KVC * BANK)
                split_kv2(1)
                take_low(piece(UKV + 3), KVC * BANK)
                mask_scores(0)
                split_kv2(2)
                split_kv2(3)
                mask_scores(1)

            def mask_scores(u):
                a = u % 2
                scale = MOBA_SCALE if u < HEADS else MLA_SCALE
                s = banks[:, 6 + a, :]
                dve.wait_ge(scores_ready, u + 1)
                if u >= 2:
                    dve.wait_ge(probs_ready, u - 1)
                nc.vector.tensor_tensor_reduce(
                    out=masked[:, a, 0:P], in0=s[:, 0:P], in1=mask[:, P:], scale=1.0, scalar=3 * MASKED,
                    op0=ALU.add, op1=ALU.max, accum_out=peak[:, a, 0:1])
                nc.vector.tensor_tensor_reduce(
                    out=masked[:, a, P:], in0=s[:, P:3 * P], in1=mask[:, :], scale=1.0, scalar=3 * MASKED,
                    op0=ALU.add, op1=ALU.max, accum_out=peak[:, a, 1:2]).then_inc(peaked, 1)
                dve.wait_ge(peaked, u + 1)
                nc.vector.tensor_scalar(shift[:, a, :], peak[:, a, :], -scale, None, ALU.mult)\
                  .then_inc(shifted, 1)

            def invert_sums(u):
                dve.wait_ge(probs_ready, u + 1)
                if u >= 2:
                    dve.wait_ge(head_out, u - 1)
                nc.vector.reciprocal(rtotal[:, u % 2, :], total[:, u % 2, :]).then_inc(totalled, 1)

            def divide_head(u):
                a = u % 2
                at = u * HD
                dve.wait_ge(totalled, u + 1)
                dve.wait_ge(head_ready, u + 1)
                for t in range(TILES):
                    ins = nc.vector.tensor_scalar(heads[:, t, at:at + HD], banks[:, 4 + a, tile_of(t)],
                                                  rtotal[:, a, t:t + 1], None, ALU.mult)
                ins.then_inc(head_out, 1)

            def take_low_half(pc, half):
                cols = slice(half * PIECE // 2, (half + 1) * PIECE // 2)
                dve.wait_ge(hi_ready, pc.index + 1)
                ins = nc.vector.tensor_tensor(w_lo[:, pc.split, cols], raw[:, pc.slot, cols],
                                              w_hi[:, pc.split, cols], ALU.subtract)
                if half == 1:
                    ins.then_inc(lo_ready, 1)

            def scale_heads(k):
                for t in range(TILES):
                    nc.vector.tensor_scalar(heads[:, t, quarter(k)], heads[:, t, quarter(k)],
                                            rs[:, R_MOBA if k < 2 else R_MLA, t:t + 1], None, ALU.mult)\
                      .then_inc(rows_ready, 1)

            def attention():
                for u in range(2, 2 * HEADS + 3):
                    if u < 2 * HEADS + 2:
                        invert_sums(u - 2)
                    if u < 2 * HEADS:
                        mask_scores(u)
                    if u >= 3:
                        divide_head(u - 3)
                    if u in (HEADS + 2, HEADS + 3):
                        take_low_half(piece(OUT), u - HEADS - 2)
                    if u in (HEADS + 6, 2 * HEADS + 1):
                        take_low_half(piece(OUT + 1), u // (2 * HEADS))
                    if u == HEADS + 4:
                        dve.wait_ge(rs_ready, rs_of(R_MOBA))
                        dve.wait_ge(head_out, HEADS)
                        scale_heads(0)
                    if u == HEADS + 5:
                        scale_heads(1)
                    if u in (HEADS + 7, HEADS + 8):
                        turn_low(2, 0, ((0, 1), (2, 3))[u - HEADS - 7])
                turn_low(2, 1)

            def mix_out():
                dve.wait_ge(rs_ready, rs_of(R_MLA))
                dve.wait_ge(head_out, 2 * HEADS)
                scale_heads(2)
                scale_heads(3)
                take_low(piece(OUT + 2))
                turn_low(2, 2)
                take_low(piece(OUT + 3))
                turn_low(2, 3)
                dve.wait_ge(gain_row_landed, 32)
                for n in range(1, OUT_BLOCKS):
                    take_low(piece(OUT + 4 * n))
                    take_low(piece(OUT + 4 * n + 1))
                    for t in range(TILES):
                        scale_out(n - 1, t)
                    take_low(piece(OUT + 4 * n + 2))
                    take_low(piece(OUT + 4 * n + 3))
                take_low(piece(GU2))

            def scale_out(n, t):
                dve.wait_ge(squared, 16 + 2 * n + t + 1)
                nc.vector.tensor_tensor(scaled[:, t, quarter(n)], result(n, t), gain_row[:, quarter(n)],
                                        ALU.mult).then_inc(y_scaled, 1)

            dve.wait_ge(first_hi_ready, 1)
            nc.vector.tensor_tensor(w_lo[:, 0, 0:PIECE // 2], raw[:, 0, 0:PIECE // 2], w_hi[:, 0, 0:PIECE // 2],
                                    ALU.subtract).then_inc(first_lo_ready, 1)
            dve.wait_ge(gains_kept, 1)
            turn_low(0, 0)
            dve.wait_ge(hi_ready, 1)
            nc.vector.tensor_tensor(w_lo[:, 0, PIECE // 2:], raw[:, 0, PIECE // 2:], w_hi[:, 0, PIECE // 2:],
                                    ALU.subtract).then_inc(lo_ready, 1)
            take_low(piece(GU1 + 1))
            turn_low(0, 1)
            take_low(piece(GU1 + 2))
            turn_low(0, 2)
            turn_low(0, 3)
            take_low(piece(GU1 + 3))
            gate_up(GU1)
            down(GU1, DOWN1, 2, 1)
            take_low(piece(IN))
            add_residual(R_POST1, 1, lambda t: scale_down(1, 4, t), IN)
            mix_in()
            latent_up()
            attention()
            mix_out()
            add_residual(R_POST_MIX, 3, lambda t: scale_out(OUT_BLOCKS - 1, t), GU2)
            gate_up(GU2)
            down(GU2, DOWN2, 26, 3)
            add_residual(R_POST2, None, lambda t: scale_down(1, 28, t))

        @block.tensor
        def _(pe):
            def three_passes(out_ap, hi, lo, rhs_hi, rhs_lo, start, stop, chain=False):
                nc.tensor.matmul(out_ap, hi, rhs_hi, start=start, stop=False, skip_group_check=chain)
                nc.tensor.matmul(out_ap, hi, rhs_lo, start=False, stop=False, skip_group_check=chain)
                return nc.tensor.matmul(out_ap, lo, rhs_hi, start=False, stop=stop, skip_group_check=chain)

            def turn(n_turn, k):
                source = heads if n_turn == 2 else rows
                if n_turn != 2 and k >= 2:
                    pe.wait_ge(act_ready, DC * n_turn + 4 * (k - 1))
                if n_turn == 2 and k == 1:
                    pe.wait_ge(peaked, 2 * HEADS)
                if n_turn == 2 and k == 3:
                    pe.wait_ge(act_ready, DC * n_turn + 8)
                for t in range(TILES):
                    pe.wait_ge(rows_ready, 8 * (n_turn - 1) + 2 * k + t + 1)
                    for j in range(4):
                        c = 4 * k + j
                        mm = nc.tensor.transpose(turn_at(n_turn, k, j)[:, tile_of(t)],
                                                 source[:, t, c * P:(c + 1) * P], ident[:, :])
                mm.then_inc(quad_turned, 1)

            def dense_piece(pc, i, blk, parity, width=BANK, n_turn=None):
                halves = isinstance(pc.index, int) and pc.index == 0
                if halves:
                    pe.wait_ge(first_lo_ready, 1)
                else:
                    pe.wait_ge(lo_ready, pc.index + 1)
                if i == 0 and not (isinstance(blk, int) and blk in (B_GU1, B_GU1 + 1)):
                    pe.wait_ge(taken, blk * 2 - 2)
                rhs_hi, rhs_lo = cut(w_hi, pc.split, 4, width), cut(w_lo, pc.split, 4, width)
                for j in range(4):
                    c = 4 * i + j
                    if halves and j == 2:
                        pe.wait_ge(lo_ready, 1)
                    if n_turn is not None:
                        pe.wait_ge(act_ready, DC * n_turn + c + 1)
                    for t in range(TILES):
                        mm = three_passes(result(parity, t)[:, 0:width], act_hi[:, c, tile_of(t)],
                                          act_lo[:, c, tile_of(t)], rhs_hi[:, j, :], rhs_lo[:, j, :],
                                          start=(c == 0), stop=(c == DC - 1))
                mm.then_inc(piece_used, 1)

            def first_block(at, blk, n_turn):
                if n_turn:
                    turn(n_turn, 0)
                    turn(n_turn, 1)
                dense_piece(piece(at), 0, blk, 0, BANK, n_turn)
                if n_turn:
                    turn(n_turn, 2)
                dense_piece(piece(at + 1), 1, blk, 0, BANK, n_turn)
                if n_turn:
                    turn(n_turn, 3)
                dense_piece(piece(at + 2), 2, blk, 0, BANK, n_turn)
                dense_piece(piece(at + 3), 3, blk, 0, BANK, n_turn)

            def turn_hidden(stage, b):
                blocks, keeps = ((B_GU1, K_GU1) if stage == GU1 else (B_GU2, K_GU2))
                if not (isinstance(b, int) and b == 0):
                    pe.wait_ge(kept, keeps + b)
                pe.wait_ge(taken, b * 2 + (2 * blocks + 2))
                for c in range(2):
                    for t in range(TILES):
                        mm = nc.tensor.transpose(banks[:, 4, c * TOKENS + t * P:c * TOKENS + (t + 1) * P],
                                                 hid[:, t, tile_of(c)], ident[:, :])
                mm.then_inc(turned, 1)

            def gate_up(stage, n_turn):
                blocks = B_GU1 if stage == GU1 else B_GU2
                first_block(stage, blocks, n_turn)
                for i in range(4):
                    dense_piece(piece(stage + 4 + i), i, blocks + 1, 1)
                    if i == 1:
                        turn_hidden(stage, 0)
                with pe.Fori(0, (N_FB - 2) // 2) as n:
                    for e in range(2):
                        for i in range(4):
                            dense_piece(piece(stage + 8 + 4 * e + i, n, 8), i, n * 2 + (blocks + 2 + e), e)
                            if i == 1:
                                turn_hidden(stage, n * 2 + (1 + e))

            def down_piece(pc, half, first=False):
                pe.wait_ge(lo_ready, pc.index + 1)
                rhs_hi, rhs_lo = cut(w_hi, pc.split, 2, D // 2), cut(w_lo, pc.split, 2, D // 2)
                for t in range(TILES):
                    b = down_banks(half, t)
                    for j in range(2):
                        hi = hid_split[:, pc.split, 0, j, tile_of(t)]
                        lo = hid_split[:, pc.split, 1, j, tile_of(t)]
                        for lhs, rhs in ((hi, rhs_hi), (hi, rhs_lo), (lo, rhs_hi)):
                            for n in range(2):
                                mm = nc.tensor.matmul(banks[:, b + n, :], lhs, rhs[:, j, quarter(n)],
                                                      start=first and j == 0 and lhs is hi and rhs is rhs_hi, stop=True, skip_group_check=True)
                    mm.then_inc(piece_used if t else tile0_done, 1)

            def down(gu_stage, stage):
                blocks, keeps = ((B_GU1, K_GU1) if gu_stage == GU1 else (B_GU2, K_GU2))
                pe.wait_ge(taken, 2 * blocks + 2 * (N_FB - 1))
                down_piece(piece(stage), 0, True)
                turn_hidden(gu_stage, N_FB - 1)
                down_piece(piece(stage + 1), 0)
                with pe.Fori(0, (HALF - 2) // 4) as i:
                    for n in range(2, 6):
                        down_piece(piece(stage + n, i, 4), 0)
                pe.wait_ge(kept, keeps + N_FB)
                for n in range(2):
                    down_piece(piece(stage + HALF + n), 1, n == 0)
                with pe.Fori(0, (HALF - 2) // 4) as i:
                    for n in range(2, 6):
                        down_piece(piece(stage + HALF + n, i, 4), 1)

            def turn_latent(first, chunks, bank, col, count):
                pe.wait_ge(taken, count)
                for c in range(chunks):
                    for t in range(TILES):
                        mm = nc.tensor.transpose(banks[:, bank + c // 2, (c % 2) * TOKENS + t * P:
                                                       (c % 2) * TOKENS + (t + 1) * P],
                                                 lat[:, t, col + c * P:col + (c + 1) * P], ident[:, :])
                return mm

            def turn_qk(j):
                pe.wait_ge(taken, j * 2 + (2 * (B_IN + 2) + 2))
                pe.wait_ge(kept, K_QK + j)
                for t in range(TILES):
                    for h in range(4):
                        mm = nc.tensor.transpose(banks[:, 4 + t, tile_of(h)], turn_in[:, t, tile_of(h)], ident[:, :])
                mm.then_inc(turned, 1)

            def mix_in():
                first_block(IN, B_IN, 1)
                for i in range(4):
                    dense_piece(piece(IN + 4 + i), i, B_IN + 1, 1, LAT)
                    if i == 1:
                        pe.wait_ge(act_ready, 2 * DC)
                        turn_latent(0, QC, 4, 0, 2 * B_IN + 2).then_inc(turned, 1)
                for i in range(4):
                    dense_piece(piece(IN + 8 + i), i, B_IN + 2, 0)
                    if i == 1:
                        turn_latent(QC, KVC, 6, Q_RANK, 2 * B_IN + 4)
                        pe.wait_ge(pe_rows, 2)
                        for t in range(TILES):
                            mm = nc.tensor.transpose(banks[0:ROPE, 7, tile_of(t)], turn_in[:, t, 0:ROPE], ident[:, :])
                        mm.then_inc(turned, 1)
                pe.wait_ge(lat_ready, QC)
                with pe.Fori(0, 2) as n:
                    for e in range(2):
                        for i in range(4):
                            dense_piece(piece(IN + 12 + 4 * e + i, n, 8), i, n * 2 + (B_IN + 3 + e), 1 - e)
                            if i == 1:
                                turn_qk(2 * n + e)
                for i in range(4):
                    dense_piece(piece(IN + 28 + i), i, B_IN + 7, 1)

            def latent_block(pc, blk, first, chunks, rhs, width):
                pe.wait_ge(lo_ready, pc.index + 1)
                pe.wait_ge(taken, 2 * blk - 2)
                rhs_hi, rhs_lo = rhs
                for c in range(chunks):
                    for t in range(TILES):
                        mm = three_passes(result(blk, t)[:, 0:width], lat_hi[:, first + c, tile_of(t)],
                                          lat_lo[:, first + c, tile_of(t)], rhs_hi[:, c, :], rhs_lo[:, c, :],
                                          start=(c == 0), stop=(c == chunks - 1))
                return mm

            def turn_q2(j):
                pe.wait_ge(taken, 2 * (B_UQ + j) + 2)
                pe.wait_ge(kept, K_UQ + j)
                for t in range(TILES):
                    for h in range(2):
                        nc.tensor.transpose(banks[:, 4 + t, tile_of(h)], turn_in[:, t, tile_of(h)], ident[:, :])
                        at = 2 * HD + h * ROPE
                        mm = nc.tensor.transpose(banks[0:ROPE, 4 + t, tile_of(2 + h)],
                                                 turn_in[:, t, at:at + ROPE], ident[:, :])
                mm.then_inc(turned, 1)

            def turn_k2(j):
                pe.wait_ge(taken, 2 * (B_UKV + j) + 2)
                pe.wait_ge(kept, K_UKV + j)
                for t in range(TILES):
                    for h in range(2):
                        mm = nc.tensor.transpose(banks[:, 4 + t, tile_of(h)], turn_in[:, t, tile_of(h)], ident[:, :])
                mm.then_inc(turned, 1)

            def latent_up():
                width = 2 * (HD + ROPE)
                for j in range(UQ_BLOCKS):
                    pc = piece(UQ + j)
                    rhs = [cut(w, pc.split, QC, width) for w in (w_hi, w_lo)]
                    latent_block(pc, B_UQ + j, 0, QC, rhs, width).then_inc(piece_used, 1)
                    if j >= 1:
                        turn_q2(j - 1)
                for j in range(UKV_BLOCKS):
                    pc = piece(UKV + j)
                    rhs = [cut(w, pc.split, KVC, BANK) for w in (w_hi, w_lo)]
                    latent_block(pc, B_UKV + j, QC, KVC, rhs, BANK).then_inc(piece_used, 1)
                    if j == 0:
                        turn_q2(UQ_BLOCKS - 1)
                    else:
                        turn_k2(j - 1)
                    if j >= 2:
                        scores(j - 2)
                scores(2)
                turn_k2(UKV_BLOCKS - 1)
                turn_probs(0)

            def scores(u):
                s = banks[:, 6 + u % 2, :]
                if u >= 2:
                    pe.wait_ge(peaked, u - 1)
                h = u % HEADS
                for t, at in ((0, slice(0, P)), (1, slice(P, 3 * P))):
                    keys = slice(0, (t + 1) * P)
                    if u < HEADS:
                        mm = nc.tensor.matmul(s[:, at], qkT[:, h, tile_of(t)], qkT[:, HEADS + h, keys],
                                              start=True, stop=True)
                    else:
                        nc.tensor.matmul(s[:, at], q2T[:, h, tile_of(t)], k2T[:, h, keys], start=True, stop=False)
                        mm = nc.tensor.matmul(s[:, at], q2pT[:, h, tile_of(t)], k2pT[:, keys], start=False, stop=True)
                mm.then_inc(scores_ready, 1)

            def turn_probs(u):
                a = u % 2
                pe.wait_ge(probs_ready, u + 1)
                if u >= 2:
                    pe.wait_ge(probs_kept, u - 1)
                for n in range(3):
                    mm = nc.tensor.transpose(banks[:, 2 + a, tile_of(n)], probs[:, a, tile_of(n)], ident[:, :])
                mm.then_inc(probs_turned, 1)

            def weigh_values(u):
                a, h = u % 2, u % HEADS
                values = v1 if u < HEADS else v2
                cols = slice(h * HD, (h + 1) * HD)
                pe.wait_ge(probs_kept, u + 1)
                if u >= 2:
                    pe.wait_ge(head_out, u - 1)
                nc.tensor.matmul(banks[:, 4 + a, 0:P], probsT[:, a, 0:P], values[:, 0, cols], start=True, stop=True)
                nc.tensor.matmul(banks[:, 4 + a, P:2 * P], probsT[:, a, P:2 * P], values[:, 0, cols],
                                 start=True, stop=False)
                nc.tensor.matmul(banks[:, 4 + a, P:2 * P], probsT[:, a, 2 * P:], values[:, 1, cols],
                                 start=False, stop=True).then_inc(head_ready, 1)

            def attention():
                for u in range(3, 2 * HEADS + 3):
                    if u == HEADS:
                        pe.wait_ge(kept, K_GU2)
                    if u < 2 * HEADS:
                        scores(u)
                    if u < 2 * HEADS + 2:
                        turn_probs(u - 2)
                    weigh_values(u - 3)
                    if u == HEADS + 5:
                        turn(2, 0)
                    if u == HEADS + 8:
                        turn(2, 1)

            def out_piece(pc, i, n, n_turn=None):
                pe.wait_ge(lo_ready, pc.index + 1)
                rhs_hi, rhs_lo = cut(w_hi, pc.split, 4, BANK), cut(w_lo, pc.split, 4, BANK)

                def chunk(j, t):
                    c = 4 * i + j
                    hi, lo = act_split(2, c)
                    return three_passes(result(n, t), hi[:, tile_of(t)], lo[:, tile_of(t)],
                                        rhs_hi[:, j, :], rhs_lo[:, j, :], start=(c == 0), stop=(c == DC - 1))
                if i < 3:
                    for j in range(4):
                        if n_turn is not None:
                            pe.wait_ge(act_ready, DC * n_turn + 4 * i + j + 1)
                        for t in range(TILES):
                            mm = chunk(j, t)
                    mm.then_inc(piece_used, 1)
                else:
                    if n_turn is not None:
                        pe.wait_ge(act_ready, DC * (n_turn + 1))
                    for t in range(TILES):
                        for j in range(4):
                            mm = chunk(j, t)
                        mm.then_inc(piece_used if t else tile0_done, 1)

            def mix_out():
                pe.wait_ge(act_ready, 2 * DC + 4)
                out_piece(piece(OUT), 0, 0)
                turn(2, 2)
                out_piece(piece(OUT + 1), 1, 0, 2)
                turn(2, 3)
                for i in range(2, 4):
                    out_piece(piece(OUT + i), i, 0, 2)
                for n in range(1, OUT_BLOCKS):
                    for i in range(4):
                        if i == 0 and n >= 2:
                            pe.wait_ge(squared, 16 + 2 * (n - 1))
                            pe.wait_ge(y_scaled, 4 + 2 * (n - 1))
                        out_piece(piece(OUT + 4 * n + i), i, n)

            pe.wait_ge(consts_made, 1)
            pe.wait_ge(gains_landed, 16)
            nc.tensor.transpose(banks[:, 7, 256:256 + G_ROWS], gain_in[:, :], ident[0:G_ROWS, 0:G_ROWS])\
              .then_inc(gains_turned, 1)
            pe.wait_ge(gains_kept, 1)
            gate_up(GU1, 0)
            down(GU1, DOWN1)
            mix_in()
            latent_up()
            attention()
            mix_out()
            gate_up(GU2, 3)
            down(GU2, DOWN2)


def rope_tables():
    parts = []
    for dim in (HD, ROPE):
        inv = (np.float32(1.0) / (np.float32(10000.0) ** (np.arange(0, dim, 2, dtype=np.float32) / np.float32(dim))))
        ang = np.arange(TOKENS, dtype=np.float32)[:, None] * inv.astype(np.float32)[None, :]
        parts += [np.cos(ang), -np.sin(ang), np.sin(ang)]
    return np.concatenate(parts, axis=1).astype(np.float32)


def lay_out_weights(w):
    stream = np.zeros((PIECES, P, PIECE), np.float32)

    def put(first, a):
        groups, cols, chunks, _, width = a.shape
        a = a.transpose(1, 0, 3, 2, 4).reshape(cols * groups, P, chunks * width)
        stream[first:first + cols * groups, :, 0:chunks * width] = a

    def cut_up(m, chunks, width):
        rows, cols = m.shape
        return m.reshape(rows // (chunks * P), chunks, P, cols // width, width).transpose(0, 3, 1, 2, 4)

    for n, gu, dn in ((1, GU1, DOWN1), (2, GU2, DOWN2)):
        gate, up = (cut_up(w[f"ffn{n}_w_{k}"][0], 4, FB) for k in ("gate", "up"))
        put(gu, np.concatenate([gate, up], axis=4))
        put(dn, cut_up(w[f"ffn{n}_w_down"][0], 2, D // 2))
    w_in = w["w_in"][0]
    rest = Q_RANK + LAT
    put(IN, cut_up(w_in[:, 0:Q_RANK], 4, BANK))
    put(IN + 4, cut_up(w_in[:, Q_RANK:rest], 4, LAT))
    put(IN + 8, cut_up(w_in[:, rest:], 4, BANK))
    put(UQ, cut_up(w["mla_w_uq"][0], QC, UQ_WIDTH))
    put(UKV, cut_up(w["mla_w_ukv"][0], KVC, BANK))
    w_out = w["w_out"][0]
    put(OUT, cut_up(np.concatenate([w_out[D // 2:], w_out[:D // 2]]), 4, BANK))
    return stream


def kernel(**inputs):
    import concourse.bacc as bacc
    from concourse.bass_utils import run_bass_kernel_spmd

    w = {name: np.asarray(a) for name, a in inputs.items()}
    x = np.ascontiguousarray(w["x"])
    gains = [w[n][0] for n in ("ffn1_pre_g", "mix_pre_g", "moba_out_g", "mla_out_g", "ffn2_pre_g",
                               "mla_q_norm_g", "mla_kv_norm_g")]
    arrays = {
        "x": x,
        "x_turned": np.ascontiguousarray(x[0].reshape(TOKENS, DC, P).transpose(2, 1, 0)),
        "weights": lay_out_weights(w),
        "gains": np.concatenate(gains).reshape(G_ROWS, P),
        "post_gains": np.concatenate([w["ffn1_post_g"], w["mix_post_g"], w["ffn2_post_g"]]),
        "rope": rope_tables(),
    }
    nc = bacc.Bacc("TRN2", target_bir_lowering=False, num_devices=1)
    args = [nc.dram_tensor(f"in_{n}", a.shape, F32, kind="ExternalInput").ap() for n, a in arrays.items()]
    args.append(nc.dram_tensor("out_rows", (1, TOKENS, D), F32, kind="ExternalOutput").ap())
    build_layer(nc, *args)
    ins = {f"in_{n}": a for n, a in arrays.items()}
    return run_bass_kernel_spmd(nc, [ins], core_ids=[0]).results[0]["out_rows"]
```
